# Optimizing a Trainium2 kernel written in Bass

```python
import math
import jax, jax.numpy as jnp
from jax import lax
import numpy as np

D_MODEL = 1024
BATCH = 1
SEQ = 512
DEPTH = 1

HEAD_DIM = 64
N_MOBA_HEADS = 6
N_FOX_HEADS = 6
CONV_CH = 256
MOBA_W = N_MOBA_HEADS * HEAD_DIM
FOX_W = N_FOX_HEADS * HEAD_DIM
MIX_W = MOBA_W + FOX_W + CONV_CH
SPLIT_SIZES = [MOBA_W, MOBA_W, MOBA_W, FOX_W, FOX_W, FOX_W, N_FOX_HEADS, CONV_CH, CONV_CH, CONV_CH]
IN_W = int(sum(SPLIT_SIZES))
SPLIT_IDX = [int(v) for v in np.cumsum(SPLIT_SIZES)[:-1]]
MOBA_BLOCK = 256
MOBA_TOPK = 3
MOBA_Q_CHUNK = 32
FOX_Q_BLOCK = 128
CONV_WIDTH = 3
REL_BUCKETS = 32
REL_MAX_DIST = 128
D_FF = -(-8 * D_MODEL // (3 * 256)) * 256
RMS_EPS = 1e-6

kernel_name = "hybrid_moba_fox_shortconv_block"

def rms_norm(x, g):
    xf = x.astype(jnp.float32)
    y = xf * lax.rsqrt(jnp.mean(xf * xf, axis=-1, keepdims=True) + RMS_EPS)
    return (y * g.astype(jnp.float32)).astype(x.dtype)

def t5_bucket(dist):
    max_exact = REL_BUCKETS // 2
    n = jnp.maximum(dist, 0)
    nf = jnp.maximum(n, 1).astype(jnp.float32)
    large = max_exact + (jnp.log(nf / max_exact) / math.log(REL_MAX_DIST / max_exact)
                         * (REL_BUCKETS - max_exact)).astype(jnp.int32)
    large = jnp.minimum(large, REL_BUCKETS - 1)
    return jnp.where(n < max_exact, n, large)

def moba_attention(q, k, v, rel_bias):
    B, H, S, Dh = q.shape
    nb = -(-S // MOBA_BLOCK)
    pad = nb * MOBA_BLOCK - S
    kp = jnp.pad(k, ((0, 0), (0, 0), (0, pad), (0, 0)))
    vp = jnp.pad(v, ((0, 0), (0, 0), (0, pad), (0, 0)))
    kb = kp.reshape(B, H, nb, MOBA_BLOCK, Dh)
    vb = vp.reshape(B, H, nb, MOBA_BLOCK, Dh)
    kmean = jnp.mean(kb.astype(jnp.float32), axis=3)
    topk = min(MOBA_TOPK, nb)
    scale = Dh ** -0.5
    rb = rel_bias.astype(jnp.float32)
    rb_t = rb.T
    b_idx = jnp.arange(B)[:, None, None, None]
    h_idx = jnp.arange(H)[None, :, None, None]
    offs = jnp.arange(MOBA_BLOCK)
    C = MOBA_Q_CHUNK
    nC = S // C
    q_chunks = q.reshape(B, H, nC, C, Dh).transpose(2, 0, 1, 3, 4)

    def chunk(args):
        qc, c = args
        t = c * C + jnp.arange(C)
        own = (c * C) // MOBA_BLOCK
        gate = jnp.einsum('bhcd,bhnd->bhcn', qc.astype(jnp.float32), kmean)
        gate = jnp.where(jnp.arange(nb) < own, gate, -jnp.inf)
        _, sel = lax.top_k(gate, topk)
        sel_ok = jnp.arange(topk) < own
        kg = kb[b_idx, h_idx, sel]
        vg = vb[b_idx, h_idx, sel]
        kpos = sel[..., None] * MOBA_BLOCK + offs
        lg = jnp.einsum('bhcd,bhcjpd->bhcjp', qc, kg).astype(jnp.float32) * scale
        lg = lg + rb_t[h_idx[..., None], t5_bucket(t[None, None, :, None, None] - kpos)]
        lg = jnp.where(sel_ok[:, None], lg, -jnp.inf)
        ko = lax.dynamic_slice_in_dim(kp, own * MOBA_BLOCK, MOBA_BLOCK, axis=2)
        vo = lax.dynamic_slice_in_dim(vp, own * MOBA_BLOCK, MOBA_BLOCK, axis=2)
        dist = t[:, None] - (own * MOBA_BLOCK + offs)[None, :]
        lo = jnp.einsum('bhcd,bhpd->bhcp', qc, ko).astype(jnp.float32) * scale
        lo = lo + jnp.transpose(rb[t5_bucket(dist)], (2, 0, 1))
        lo = jnp.where(dist >= 0, lo, -jnp.inf)
        logits = jnp.concatenate([lo, lg.reshape(B, H, C, topk * MOBA_BLOCK)], axis=-1)
        p = jax.nn.softmax(logits, axis=-1).astype(v.dtype)
        po = p[..., :MOBA_BLOCK]
        pg = p[..., MOBA_BLOCK:].reshape(B, H, C, topk, MOBA_BLOCK)
        return (jnp.einsum('bhcp,bhpd->bhcd', po, vo)
                + jnp.einsum('bhcjp,bhcjpd->bhcd', pg, vg))

    out = lax.map(chunk, (q_chunks, jnp.arange(nC)))
    return out.transpose(1, 2, 0, 3, 4).reshape(B, H, S, Dh)

def forgetting_attention(q, k, v, log_f):
    B, H, S, Dh = q.shape
    scale = Dh ** -0.5
    cum = lax.cumsum(log_f, axis=2)
    nQ = S // FOX_Q_BLOCK
    qb = q.reshape(B, H, nQ, FOX_Q_BLOCK, Dh).transpose(2, 0, 1, 3, 4)
    cb = cum.reshape(B, H, nQ, FOX_Q_BLOCK).transpose(2, 0, 1, 3)
    kpos = jnp.arange(S)

    def blk(args):
        qi, ci, i = args
        t = i * FOX_Q_BLOCK + jnp.arange(FOX_Q_BLOCK)
        lg = (jnp.einsum('bhqd,bhsd->bhqs', qi, k).astype(jnp.float32) * scale
              + ci[..., None] - cum[:, :, None, :])
        lg = jnp.where(kpos[None, :] <= t[:, None], lg, -jnp.inf)
        p = jax.nn.softmax(lg, axis=-1).astype(v.dtype)
        return jnp.einsum('bhqs,bhsd->bhqd', p, v)

    out = lax.map(blk, (qb, cb, jnp.arange(nQ)))
    return out.transpose(1, 2, 0, 3, 4).reshape(B, H, S, Dh)

def short_conv_mixer(gate_b, gate_c, h, conv_w):
    u = gate_c * h
    y = lax.conv_general_dilated(u, conv_w[:, None, :].astype(u.dtype), window_strides=(1,),
                                 padding=[(CONV_WIDTH - 1, 0)],
                                 dimension_numbers=('NWC', 'WIO', 'NWC'),
                                 feature_group_count=CONV_CH)
    return gate_b * y

def hybrid_layer(x, w_in, b_f, conv_w, w_out, rel_bias, g_pre_mix, g_post_mix,
                 g_pre_ffn, g_post_ffn, w_gate, w_up, w_down):
    B, S, _ = x.shape
    hn = rms_norm(x, g_pre_mix)
    proj = hn @ w_in
    mq, mk, mv, fq, fk, fv, f_logit, cvb, cvc, cvh = jnp.split(proj, SPLIT_IDX, axis=-1)

    def heads(t, n):
        return t.reshape(B, S, n, HEAD_DIM).transpose(0, 2, 1, 3)

    def merge(o):
        return o.transpose(0, 2, 1, 3).reshape(B, S, -1)

    moba = moba_attention(heads(mq, N_MOBA_HEADS), heads(mk, N_MOBA_HEADS),
                          heads(mv, N_MOBA_HEADS), rel_bias)
    log_f = jax.nn.log_sigmoid((f_logit + b_f).astype(jnp.float32)).transpose(0, 2, 1)
    fox = forgetting_attention(heads(fq, N_FOX_HEADS), heads(fk, N_FOX_HEADS),
                               heads(fv, N_FOX_HEADS), log_f)
    conv = short_conv_mixer(cvb, cvc, cvh, conv_w)
    mixed = jnp.concatenate([merge(moba), merge(fox), conv], axis=-1) @ w_out
    x = x + rms_norm(mixed, g_post_mix)
    h2 = rms_norm(x, g_pre_ffn)
    ff = (jax.nn.silu(h2 @ w_gate) * (h2 @ w_up)) @ w_down
    return x + rms_norm(ff, g_post_ffn)

def setup_inputs(seed: int = 0) -> dict:
    key = jax.random.key(seed)
    ks = jax.random.split(key, 14)
    f32 = jnp.float32
    nrm = lambda k, shape, s: (jax.random.normal(k, shape, f32) * s).astype(f32)
    return {
        "x": nrm(ks[0], (BATCH, SEQ, D_MODEL), 1.0),
        "w_in": nrm(ks[1], (DEPTH, D_MODEL, IN_W), D_MODEL ** -0.5),
        "b_f": 2.0 + nrm(ks[2], (DEPTH, N_FOX_HEADS), 0.1),
        "conv_w": nrm(ks[3], (DEPTH, CONV_WIDTH, CONV_CH), CONV_WIDTH ** -0.5),
        "w_out": nrm(ks[4], (DEPTH, MIX_W, D_MODEL), MIX_W ** -0.5),
        "rel_bias": nrm(ks[5], (REL_BUCKETS, N_MOBA_HEADS), 0.5),
        "g_pre_mix": 1.0 + nrm(ks[6], (DEPTH, D_MODEL), 0.05),
        "g_post_mix": 1.0 + nrm(ks[7], (DEPTH, D_MODEL), 0.05),
        "g_pre_ffn": 1.0 + nrm(ks[8], (DEPTH, D_MODEL), 0.05),
        "g_post_ffn": 1.0 + nrm(ks[9], (DEPTH, D_MODEL), 0.05),
        "w_gate": nrm(ks[10], (DEPTH, D_MODEL, D_FF), D_MODEL ** -0.5),
        "w_up": nrm(ks[11], (DEPTH, D_MODEL, D_FF), D_MODEL ** -0.5),
        "w_down": nrm(ks[12], (DEPTH, D_FF, D_MODEL), D_FF ** -0.5),
    }

def reference(x, w_in, b_f, conv_w, w_out, rel_bias, g_pre_mix, g_post_mix,
              g_pre_ffn, g_post_ffn, w_gate, w_up, w_down):
    for l in range(DEPTH):
        x = hybrid_layer(x, w_in[l], b_f[l], conv_w[l], w_out[l], rel_bias,
                         g_pre_mix[l], g_post_mix[l], g_pre_ffn[l], g_post_ffn[l],
                         w_gate[l], w_up[l], w_down[l])
    return x


_drawn_inputs = setup_inputs


def setup_inputs(seed=0):
    import zlib

    import numpy as np

    out = dict(_drawn_inputs(seed))
    spreads = {}
    factors = {'b_f': 18.787}
    for name, (base, spread) in spreads.items():
        noise = np.random.default_rng([zlib.crc32(name.encode()), seed]).standard_normal(out[name].shape)
        drawn = base * np.exp(spread * noise) if base else spread * noise
        out[name] = __import__('jax').numpy.asarray(drawn.astype(out[name].dtype))
    for name, factor in factors.items():
        out[name] = (out[name] * factor).astype(out[name].dtype)
    return out
```

```python
from contextlib import ExitStack

import concourse.bass as bass
from concourse import mybir

ALU = mybir.AluOpType
ACT = mybir.ActivationFunctionType
F32 = mybir.dt.float32
F32R = mybir.dt.float32r
BF16 = mybir.dt.bfloat16

P = 128
SEQ = 512
D = 1024
TT = SEQ // P
KT = D // P
DH = 64
N_MOBA = 6
N_FOX = 6
PAIRS = (N_MOBA + N_FOX) // 2
MOBA_PAIRS = N_MOBA // 2
CONV_CH = 256
D_FF = 2816
FT = D_FF // P
MOBA_W = N_MOBA * DH
FOX_W = N_FOX * DH
EPS = 1e-6
SCALE = DH ** -0.5
MASKED = -1.0e30
BUCKETS = 32
REL = 640

U_WOUT = 24
U_GU = U_WOUT + KT
U_DOWN = U_GU + 2 * FT
WOUT_ORDER = [6, 0, 1, 2, 3, 4, 7, 5]
RAW = 4
LOOP_DOWN = 16
LAST = FT - LOOP_DOWN

PROJ = (0, 1)
SBANK = (2, 3)
TBANK = (4, 5)
OBANK = 6
VTBANK = 7
GU_BANKS = ((6, 7), (4, 5))
DOWN_BANKS = (0, 2, 6, 4)

STEPS = 8 * PAIRS


def group(p, j):
    return j if p == 0 else 4 + 3 * (p - 1) + j


F_GROUP = 3
CONV_GROUP = group(PAIRS, 0)
GROUPS = CONV_GROUP + 6


def unit_group(u):
    return group(u // 3, u % 3)


def finished(g):
    p, s = divmod(g, 8)
    if p < PAIRS - 1:
        return [group(p + 1, j) for j in range(3) if (8 * j + 7) // 3 == s]
    if p == PAIRS - 1:
        return [CONV_GROUP + m for m in range(6) if (8 * m + 7) // 6 == s]
    return []


def splits_at(g):
    p, s = divmod(g, 8)
    if p < PAIRS - 1:
        return {1: [3 * (p + 1) + 1], 4: [3 * (p + 1) + 2], 6: [3 * (p + 2)]}.get(s, [])
    return [3 * PAIRS + 1 + g - 8 * (PAIRS - 1)] if g <= STEPS else []


def hybrid_block(nc, x, w_in_units, w_f, b_f, conv_w, w_out, rel_bias, bucket_onehot, g_pre_mix, g_post_mix,
                 g_pre_ffn, g_post_ffn, w_gate_units, w_up_units, w_down, out):
    rel_rows = nc.dram_tensor("rel_rows", (N_MOBA, REL), F32, kind="Internal")
    cum_rows = nc.dram_tensor("cum_rows", (N_FOX, SEQ), F32, kind="Internal")

    with ExitStack() as ctx:
        def sem(name):
            return ctx.enter_context(nc.semaphore(name))

        base = (nc.sbuf_base + 63) // 64 * 64
        KB = 1024

        def at(name, offset, shape, dt=F32):
            return nc.alloc_sbuf_tensor_at(name, shape, dt, offset=base + offset)

        o = 0
        x_sb = at("x_sb", o, [P, TT, D]); o += 16 * KB
        hn_hi = at("hn_hi", o, [P, KT, SEQ], F32R)
        hn_lo = at("hn_lo", o + 16 * KB, [P, KT, SEQ], F32R)
        act_hi = at("act_hi", o, [P, 2, SEQ], F32R)
        act_lo = at("act_lo", o + 4 * KB, [P, 2, SEQ], F32R)
        lact_hi = at("lact_hi", o + 8 * KB, [P, LAST, SEQ], F32R)
        lact_lo = at("lact_lo", o + 20 * KB, [P, LAST, SEQ], F32R); o += 32 * KB
        cat_hi = at("cat_hi", o, [P, KT, SEQ], F32R)
        cat_lo = at("cat_lo", o + 16 * KB, [P, KT, SEQ], F32R)
        last_hi = [at(f"last_hi{n}", o + 8 * KB * n, [P, KT, P], F32R) for n in range(4)]
        last_lo = [at(f"last_lo{n}", o + 8 * KB * n + 4 * KB, [P, KT, P], F32R) for n in range(4)]
        o += 32 * KB
        raw = [at(f"raw{n}", o + 4 * KB * n, [P, KT, P]) for n in range(RAW)]; o += 4 * KB * RAW
        w_hi = [at(f"w_hi{n}", o + 8 * KB * n, [P, KT, P], F32R) for n in range(4)]
        w_lo = [at(f"w_lo{n}", o + 8 * KB * n + 4 * KB, [P, KT, P], F32R) for n in range(4)]; o += 32 * KB
        a = o
        v_hi, v_lo = [None] * 2, [None] * 2
        v_hi[0] = at("v_hi0", a, [P, TT, 3, DH], F32R)
        v_lo[0] = at("v_lo0", a + 3 * KB, [P, TT, 3, DH], F32R)
        vT = at("vT", a + 6 * KB, [P, SEQ])
        logits = at("logits", a + 8 * KB, [P, 2, SEQ])
        probs = at("probs", a + 12 * KB, [P, 2, SEQ])
        pT_hi = at("pT_hi", a + 16 * KB, [P, TT, SEQ], F32R)
        pT_lo = at("pT_lo", a + 24 * KB, [P, TT, SEQ], F32R)
        xn = at("xn", a + 16 * KB, [P, TT, D])
        squares = at("squares", a, [P, D])
        q_hl, q_lh, k_hl = [None] * 2, [None] * 2, [None] * 2
        for s in range(2):
            q_hl[s] = at(f"q_hl{s}", a + (32 + 12 * s) * KB, [P, 2, SEQ], F32R)
            q_lh[s] = at(f"q_lh{s}", a + (36 + 12 * s) * KB, [P, 2, SEQ], F32R)
            k_hl[s] = at(f"k_hl{s}", a + (40 + 12 * s) * KB, [P, 2, SEQ], F32R)
        conv_c = at("conv_c", a + 32 * KB, [P, SEQ])
        conv_y = at("conv_y", a + 34 * KB, [P, SEQ])
        conv_o = at("conv_o", a + 36 * KB, [P, SEQ])
        conv_u = at("conv_u", a + 38 * KB, [P, 2 + SEQ])
        v_hi[1] = at("v_hi1", a + 56 * KB, [P, TT, 3, DH], F32R)
        v_lo[1] = at("v_lo1", a + 59 * KB, [P, TT, 3, DH], F32R)
        bias = at("bias", a + 62 * KB, [P, 2, 2, SEQ])
        ext_hi = [at(f"ext_hi{n}", a + 8 * KB * n, [P, KT, P], F32R) for n in range(4)]
        ext_lo = [at(f"ext_lo{n}", a + 8 * KB * n + 4 * KB, [P, KT, P], F32R) for n in range(4)]
        fst_hi = [at(f"fst_hi{n}", a + (32 + 8 * n) * KB, [P, KT, P], F32R) for n in range(2)]
        fst_lo = [at(f"fst_lo{n}", a + (36 + 8 * n) * KB, [P, KT, P], F32R) for n in range(2)]
        mix_y = at("mix_y", a + 48 * KB, [P, 2, D])
        g_post_mix_b = at("g_post_mix_b", a + 56 * KB, [P, D])
        g_pre_ffn_b = at("g_pre_ffn_b", a + 60 * KB, [P, D])
        mix_sq = at("mix_sq", a + 64 * KB, [P, D])
        act = at("act", a, [P, FT, SEQ])
        silu_g = at("silu_g", a + 44 * KB, [P, 2, SEQ])
        for n in range(2):
            last_hi.append(at(f"last_hi{4 + n}", a + (48 + 8 * n) * KB, [P, KT, P], F32R))
            last_lo.append(at(f"last_lo{4 + n}", a + (52 + 8 * n) * KB, [P, KT, P], F32R))
        g_post_ffn_b = at("g_post_ffn_b", a + 64 * KB, [P, D])
        ff_y = at("ff_y", a, [P, TT, D])
        ff_sq = at("ff_sq", a + 16 * KB, [P, D])
        o = a + 70 * KB
        ident = at("ident", o, [P, P]); o += 512
        ident_b = at("ident_b", o, [P, P], BF16); o += 256
        mask_b = at("mask_b", o, [P, P], BF16); o += 256
        g_mix_c = at("g_mix_c", o, [P, KT]); o += 32
        conv_w_c = at("conv_w_c", o, [P, 2, 3]); o += 32
        wf_raw = at("wf_raw", o, [P, KT, N_FOX]); o += 192
        wf_hi = at("wf_hi", o, [P, KT, N_FOX], F32R); o += 192
        wf_lo = at("wf_lo", o, [P, KT, N_FOX], F32R); o += 192
        eps = at("eps", o, [P, 1]); o += 32
        bf_c = at("bf_c", o, [N_FOX, 1]); o += 32
        relb = at("relb", o, [BUCKETS, N_MOBA]); o += 32
        sumsq = at("sumsq", o, [P, 4, TT]); o += 64
        std = at("std", o, [P, 4, TT]); o += 64
        rstd = at("rstd", o, [P, 4, TT]); o += 64
        neg_max = at("neg_max", o, [P, STEPS]); o += 192
        row_sum = at("row_sum", o, [P, STEPS]); o += 192
        row_inv = at("row_inv", o, [P, STEPS]); o += 192
        assert base + o <= nc.sbuf_usable_end, (base + o, nc.sbuf_usable_end)
        onehot = at("onehot", a + 62 * KB, [BUCKETS, REL])
        rel_row = at("rel_row", a + 65 * KB, [N_MOBA, REL])
        f_z = at("f_z", a + 16 * KB, [N_FOX, SEQ])
        f_abs = at("f_abs", a + 8 * KB, [N_FOX, SEQ])
        f_log = at("f_log", a + 10 * KB, [N_FOX, SEQ])
        f_one = at("f_one", a + 12 * KB, [N_FOX, SEQ])
        f_cum = at("f_cum", 74 * KB, [N_FOX, SEQ])

        bank = ctx.enter_context(nc.psum_tensor("bank", [P, 8, SEQ], F32))

        x_in = [sem(f"x_in{t}") for t in range(TT)]
        tables_in = sem("tables_in")
        small_in = sem("small_in")
        raw_in = [sem(f"raw_in{n}") for n in range(RAW)]
        bias_in = [sem(f"bias_in{n}") for n in range(2)]
        rel_out = sem("rel_out")
        cum_out = sem("cum_out")
        g_mix_in = sem("g_mix_in")
        g_ffn_in = sem("g_ffn_in")
        out_done = sem("out_done")
        consts_done = sem("consts_done")
        rel_done = sem("rel_done")
        rel_copied = sem("rel_copied")
        sq_done = sem("sq_done")
        std_done = sem("std_done")
        rstd_done = sem("rstd_done")
        xn_done = sem("xn_done")
        xT_done = sem("xT_done")
        hn_hi_done = sem("hn_hi_done")
        hn_lo_done = sem("hn_lo_done")
        hi_done = sem("hi_done")
        lo_done = sem("lo_done")
        wf_hi_done = sem("wf_hi_done")
        wf_lo_done = sem("wf_lo_done")
        proj_done = sem("proj_done")
        proj_hi = sem("proj_hi")
        proj_read = sem("proj_read")
        swapped = sem("swapped")
        vT_done = sem("vT_done")
        v_hi_done = sem("v_hi_done")
        v_lo_done = sem("v_lo_done")
        f_z_done = sem("f_z_done")
        f_log_done = sem("f_log_done")
        f_cum_done = sem("f_cum_done")
        s_done = sem("s_done")
        biased = sem("biased")
        exp_done = sem("exp_done")
        inv_done = sem("inv_done")
        normed = sem("normed")
        t_done = sem("t_done")
        pT_hi_done = sem("pT_hi_done")
        pT_lo_done = sem("pT_lo_done")
        pv_done = sem("pv_done")
        o_hi = sem("o_hi")
        o_lo = sem("o_lo")
        conv_step = sem("conv_step")
        conv_hi = sem("conv_hi")
        conv_lo = sem("conv_lo")
        mix_unit_used = sem("mix_unit_used")
        mix_done = sem("mix_done")
        mix_normed = sem("mix_normed")
        x1_done = sem("x1_done")
        h2_done = sem("h2_done")
        h2T_done = sem("h2T_done")
        h2_hi = sem("h2_hi")
        h2_lo = sem("h2_lo")
        gate_done = sem("gate_done")
        up_done = sem("up_done")
        silu_done = sem("silu_done")
        act_done = sem("act_done")
        act_hi_done = sem("act_hi_done")
        act_lo_done = sem("act_lo_done")
        down_done = sem("down_done")
        down_tile = sem("down_tile")
        ff_normed = sem("ff_normed")
        y_done = sem("y_done")

        SQ1, SQ2, SQ3, SQ4 = range(4)

        def norm_no(n, t):
            return {SQ1: t + 1, SQ2: TT + 2 * t + 1, SQ3: TT + 2 * t + 2, SQ4: 3 * TT + t + 1}[n]

        def split_slot(u):
            if U_WOUT + 4 <= u < U_GU:
                return ext_hi[u - U_WOUT - 4], ext_lo[u - U_WOUT - 4]
            if U_GU <= u < U_GU + 2:
                return fst_hi[u - U_GU], fst_lo[u - U_GU]
            if u >= U_DOWN + LOOP_DOWN:
                return last_hi[u - U_DOWN - LOOP_DOWN], last_lo[u - U_DOWN - LOOP_DOWN]
            return w_hi[u % 4], w_lo[u % 4]

        block = ctx.enter_context(nc.Block())

        @block.sync
        def _(sp):
            def load(u, src, free_value=None):
                if free_value is not None:
                    sp.wait_ge(lo_done, free_value)
                sp.dma_start(raw[u % RAW][:, :, :], src).then_inc(raw_in[u % RAW], 16)

            def unit(w, n):
                return w[n].rearrange("p (k n) -> p k n", n=P)

            def rows(w, k):
                return w[P * k:P * (k + 1), :].rearrange("p (k n) -> p k n", n=P)

            for t in range(TT):
                sp.dma_start(x_sb[:, t, :], x[P * t:P * (t + 1), :]).then_inc(x_in[t], 16)
            for u in range(U_WOUT):
                load(u, unit(w_in_units, u), u - RAW + 1 if u >= RAW else None)
            for n, k in enumerate(WOUT_ORDER):
                load(U_WOUT + n, rows(w_out, k), U_WOUT + n - RAW + 1)
            with sp.Fori(0, FT // 2) as i:
                for j in range(4):
                    w = (w_gate_units, w_up_units)[j % 2]
                    load(U_GU + j, w[bass.ds(i * 2 + j // 2, 1)].rearrange("o p (k n) -> (o p) k n", n=P),
                         i * 4 + (U_GU + j - RAW + 1))
            with sp.Fori(0, LOOP_DOWN // 4) as i:
                for j in range(4):
                    load(U_DOWN + j, w_down[bass.ds(i * (4 * P) + P * j, P), :].rearrange("p (k n) -> p k n", n=P),
                         i * 4 + (U_DOWN + j - RAW + 1))
            for f in range(LOOP_DOWN, FT):
                load(U_DOWN + f, rows(w_down, f), U_DOWN + f - RAW + 1)
            for t in range(TT):
                sp.wait_ge(y_done, t + 1)
                sp.dma_start(out[P * t:P * (t + 1), :], ff_y[:, t, :]).then_inc(out_done, 16)
            sp.wait_ge(out_done, 16 * TT)

        @block.gpsimd
        def _(pool):
            pool.dma_start(relb[:, :], rel_bias).then_inc(tables_in, 16)
            pool.dma_start(onehot[:, :], bucket_onehot).then_inc(tables_in, 16)
            pool.dma_start(g_mix_c[:, :], g_pre_mix).then_inc(small_in, 16)
            pool.dma_start(bf_c[:, :], b_f).then_inc(small_in, 16)
            pool.dma_start(conv_w_c[:, :, :], conv_w).then_inc(small_in, 16)
            pool.dma_start(wf_raw[:, :, :], w_f).then_inc(small_in, 16)
            nc.gpsimd.memset(ident[:, :], 1.0).then_inc(consts_done, 1)
            nc.gpsimd.memset(ident_b[:, :], 1.0).then_inc(consts_done, 1)
            nc.gpsimd.memset(mask_b[:, :], 0.0).then_inc(consts_done, 1)
            nc.gpsimd.memset(eps[:, :], EPS).then_inc(consts_done, 1)
            pool.wait_ge(consts_done, 3)
            for m in (ident, ident_b):
                nc.gpsimd.affine_select(out=m[:, :], in_=m[:, :], compare_op=ALU.is_equal, fill=0.0, base=0,
                                        pattern=[[-1, P]], channel_multiplier=1).then_inc(consts_done, 1)
            nc.gpsimd.affine_select(out=mask_b[:, :], in_=mask_b[:, :], compare_op=ALU.is_ge, fill=MASKED, base=0,
                                    pattern=[[-1, P]], channel_multiplier=1).then_inc(consts_done, 1)
            nc.gpsimd.memset(f_one[:, :], 1.0).then_inc(consts_done, 1)
            pool.wait_ge(sq_done, TT)
            for m in (v_hi[0], v_lo[0], v_hi[1], v_lo[1]):
                nc.gpsimd.memset(m[:, :, 1, :].bitcast(F32), 0.0).then_inc(consts_done, 1)

            pool.wait_ge(rel_copied, 2)
            pool.dma_start(rel_rows.ap(), rel_row[:, :]).then_inc(rel_out, 16)

            for p in range(PAIRS):
                s = p % 2
                if p == 0:
                    pool.wait_ge(rel_out, 16)
                if p == MOBA_PAIRS:
                    pool.wait_ge(cum_out, 16)
                if p >= 2:
                    pool.wait_ge(biased, 8 * (p - 1))
                for h in range(2):
                    if p < MOBA_PAIRS:
                        src = bass.AP(rel_rows, (2 * p + h) * REL, [[1, P], [1, SEQ]])
                    else:
                        src = bass.AP(cum_rows, (2 * (p - MOBA_PAIRS) + h) * SEQ, [[0, P], [1, SEQ]])
                    pool.dma_start(bias[:, s, h, :], src).then_inc(bias_in[s], 16)
                pool.wait_ge(proj_read, group(p, 0) + 1)
                if p == 0:
                    pool.wait_ge(consts_done, 11)
                for n in range(4):
                    h, to = divmod(n, 2)
                    if 4 * p + n:
                        pool.wait_ge(swapped, 4 * p + n)
                    nc.gpsimd.tensor_copy(q_lh[s][DH * to:DH * (to + 1), h, :],
                                          q_hl[s][DH - DH * to:P - DH * to, h, :]).then_inc(swapped, 1)
                if p == 0:
                    pool.wait_ge(f_cum_done, 1)
                    pool.dma_start(cum_rows.ap(), f_cum[:, :]).then_inc(cum_out, 16)

            pool.wait_ge(pv_done, 2 * PAIRS)
            pool.wait_ge(biased, STEPS)
            pool.dma_start(g_post_mix_b[:, :], g_post_mix.partition_broadcast(P)).then_inc(g_mix_in, 16)
            pool.dma_start(g_pre_ffn_b[:, :], g_pre_ffn.partition_broadcast(P)).then_inc(g_mix_in, 16)
            pool.wait_ge(sq_done, 3 * TT)
            pool.dma_start(g_post_ffn_b[:, :], g_post_ffn.partition_broadcast(P)).then_inc(g_ffn_in, 16)

        @block.scalar
        def _(act_e):
            def split(u, value=None):
                hi, _ = split_slot(u)
                v = u if value is None else value
                act_e.wait_ge(raw_in[u % RAW], 16 * (v // RAW + 1) if value is None else value)
                nc.scalar.copy(hi[:, :, :], raw[u % RAW][:, :, :]).then_inc(hi_done, 1)

            def sum_squares(n, t, src, junk):
                nc.scalar.activation(junk, src, ACT.Square, accum_out=sumsq[:, n, t:t + 1]).then_inc(sq_done, 1)
                act_e.wait_ge(sq_done, norm_no(n, t))
                nc.scalar.activation(std[:, n, t:t + 1], sumsq[:, n, t:t + 1], ACT.Sqrt, bias=eps[:, :],
                                     scale=1.0 / D).then_inc(std_done, 1)

            act_e.wait_ge(consts_done, 4)
            for t in range(TT):
                act_e.wait_ge(x_in[t], 16)
                sum_squares(SQ1, t, x_sb[:, t, :], squares[:, :])
            split(0)
            act_e.wait_ge(small_in, 64)
            for k in range(KT):
                act_e.wait_ge(xT_done, k + 1)
                nc.scalar.activation(hn_hi[:, k, :], bank[:, 2 + k % 6, :], ACT.Copy,
                                     scale=g_mix_c[:, k:k + 1]).then_inc(hn_hi_done, 1)
            split(1)
            split(2)
            nc.scalar.copy(wf_hi[:, :, :], wf_raw[:, :, :]).then_inc(wf_hi_done, 1)
            split(3)

            def evac_hi(G):
                if G == F_GROUP or G >= CONV_GROUP:
                    return
                p, j = (0, G) if G < 3 else ((G - 4) // 3 + 1, (G - 4) % 3)
                if j == 2:
                    return
                act_e.wait_ge(proj_done, G + 1)
                if p >= 2 and j == 0:
                    act_e.wait_ge(s_done, 8 * (p - 1))
                dst = (q_hl, k_hl)[j][p % 2]
                for h in range(2):
                    last = nc.scalar.activation(dst[0:DH, h, :], bank[DH * h:DH * (h + 1), PROJ[G % 2], :], ACT.Copy,
                                                scale=SCALE if j == 0 else 1.0)
                last.then_inc(proj_hi, 1)

            def evac_v(p):
                act_e.wait_ge(vT_done, p + 1)
                if p >= 2:
                    act_e.wait_ge(pv_done, 2 * (p - 1))
                nc.scalar.copy(v_hi[p % 2][:, :, 0:3:2, :],
                               bank[:, VTBANK, :].rearrange("p (j h d) -> p j h d", j=TT, h=2)).then_inc(v_hi_done, 1)

            def evac_pT(g):
                i = g % 4
                act_e.wait_ge(t_done, g + 1)
                if g >= 4:
                    act_e.wait_ge(pv_done, g // 4)
                nc.scalar.copy(pT_hi[:, 0:i + 1, P * i:P * (i + 1)],
                               bank[:, TBANK[g % 2], 0:P * (i + 1)].rearrange("p (j q) -> p j q", q=P)
                               ).then_inc(pT_hi_done, 1)

            def evac_o(p):
                act_e.wait_ge(pv_done, 2 * p + 2)
                nc.scalar.copy(cat_hi[:, p, :], bank[:, OBANK, :]).then_inc(o_hi, 1)

            def forget_log():
                act_e.wait_ge(f_z_done, 2)
                nc.scalar.activation(f_abs[:, :], f_abs[:, :], ACT.Exp, scale=-1.0).then_inc(f_log_done, 1)
                act_e.wait_ge(f_log_done, 1)
                nc.scalar.activation(f_log[:, :], f_abs[:, :], ACT.Ln, bias=1.0).then_inc(f_log_done, 1)

            evac_hi(group(0, 0))
            evac_hi(group(0, 1))
            forget_log()

            conv_hi_at = {5: 0, 8: 1}
            for g in range(STEPS + 2):
                p, s = divmod(g, 8)
                if g < STEPS:
                    act_e.wait_ge(biased, g + 1)
                    if g >= 2:
                        act_e.wait_ge(t_done, g - 1)
                    n = P * (g % 4 + 1)
                    nc.scalar.activation(probs[:, g % 2, 0:n], logits[:, g % 2, 0:n], ACT.Exp, scale=-1.0,
                                         bias=neg_max[:, g:g + 1], accum_out=row_sum[:, g:g + 1]
                                         ).then_inc(exp_done, 1)
                for u in splits_at(g):
                    if 4 <= u:
                        act_e.wait_ge(proj_done, unit_group(u - 4) + 1)
                    split(u)
                if g >= 1:
                    for G in finished(g - 1):
                        evac_hi(G)
                if p < PAIRS and s == 2:
                    evac_v(p)
                if 1 <= g <= STEPS:
                    evac_pT(g - 1)
                if g >= 9 and (g - 9) % 8 == 1:
                    evac_o((g - 9) // 8)
                if g - 8 * (PAIRS - 1) in conv_hi_at:
                    c = conv_hi_at[g - 8 * (PAIRS - 1)]
                    act_e.wait_ge(proj_read, CONV_GROUP + 3 * c + 3)
                    nc.scalar.copy(cat_hi[:, 6 + c, :], conv_o[:, :]).then_inc(conv_hi, 1)
            act_e.wait_ge(pv_done, 2 * PAIRS - 2)
            split(U_WOUT + 4)
            act_e.wait_ge(t_done, STEPS)
            split(U_WOUT + 5)
            evac_o(PAIRS - 1)
            split(U_WOUT + 6)
            split(U_WOUT + 7)
            split(U_GU)
            split(U_GU + 1)

            def evac_h2(t):
                for b in range(2):
                    act_e.wait_ge(h2T_done, 2 * t + b + 1)
                    nc.scalar.copy(hn_hi[:, 4 * b:4 * b + 4, P * t:P * (t + 1)],
                                   bank[:, TBANK[b], :].rearrange("p (k q) -> p k q", q=P)).then_inc(h2_hi, 1)

            for t in range(TT):
                if t == TT - 1:
                    for n in range(2):
                        act_e.wait_ge(mix_unit_used, 3 + n)
                        split(U_GU + 2 + n)
                if t >= 1:
                    evac_h2(t - 1)
                act_e.wait_ge(mix_done, t + 1)
                b = 2 * (t % 2)
                sum_squares(SQ2, t, bank[:, b:b + 2, :].rearrange("p a n -> p (a n)"), mix_sq[:, :])
                act_e.wait_ge(x1_done, t + 1)
                sum_squares(SQ3, t, x_sb[:, t, :], mix_sq[:, :])
            evac_h2(TT - 1)

            def silu(f, par):
                act_e.wait_ge(gate_done, f + 1)
                if isinstance(f, int) and f == 0:
                    act_e.wait_ge(up_done, 1)
                if not isinstance(f, int) or f >= 2:
                    act_e.wait_ge(act_done, f - 1)
                nc.scalar.activation(silu_g[:, par, :], bank[:, GU_BANKS[par][0], :], ACT.Silu).then_inc(silu_done, 1)

            def split_gu(f, par):
                act_e.wait_ge(up_done, f + 1)
                for n in range(2):
                    u = U_GU + 4 + 2 * par + n
                    split(u, f * 8 + (16 * (u // RAW + 1) - 8 * par))

            for f in range(2):
                silu(f, f)
                split_gu(f, f)
            with act_e.Fori(1, FT // 2) as i:
                for par in range(2):
                    silu(i * 2 + par, par)
                    split_gu(i * 2 + par, par)

            def act_split(f, n):
                dst = act_hi[:, n, :] if n < 2 else lact_hi[:, n - 2, :]
                nc.scalar.copy(dst, act[:, f, :]).then_inc(act_hi_done, 1)

            act_e.wait_ge(act_done, FT)
            act_e.wait_ge(up_done, FT)
            act_split(0, 0)
            act_split(1, 1)

            def down_turn(i, j):
                act_e.wait_ge(down_done, i * 4 + (j + 1))
                split(U_DOWN + 4 + j, i * 16 + 16 * ((U_DOWN + 4) // RAW + 1))
                if isinstance(i, int):
                    act_split(4 * i + j + 2, j % 2)
                else:
                    nc.scalar.copy(act_hi[:, j % 2, :], act[:, bass.ds(i * 4 + (j + 2), 1), :].rearrange(
                        "p o n -> p (o n)")).then_inc(act_hi_done, 1)

            with act_e.Fori(0, LOOP_DOWN // 4 - 1) as i:
                for j in range(4):
                    down_turn(i, j)
            for n in range(2):
                f = LOOP_DOWN - 4 + n
                act_e.wait_ge(down_done, f + 1)
                act_split(f + 2, n)
                split(U_DOWN + LOOP_DOWN + n)
            for n in range(LAST):
                act_split(LOOP_DOWN + n, 2 + n)
                if n + 2 < LAST:
                    split(U_DOWN + LOOP_DOWN + n + 2)

            for t in range(TT):
                act_e.wait_ge(down_tile, t + 1)
                b = DOWN_BANKS[t]
                sum_squares(SQ4, t, bank[:, b:b + 2, :].rearrange("p a n -> p (a n)"), ff_sq[:, :])

        @block.vector
        def _(dve):
            def split(u, value=None):
                hi, lo = split_slot(u)
                dve.wait_ge(hi_done, u + 1 if value is None else value)
                nc.vector.tensor_tensor(lo[:, :, :], raw[u % RAW][:, :, :], hi[:, :, :],
                                        ALU.subtract).then_inc(lo_done, 1)

            def inverse_std(n, t):
                dve.wait_ge(std_done, norm_no(n, t))
                nc.vector.reciprocal(rstd[:, n, t:t + 1], std[:, n, t:t + 1]).then_inc(rstd_done, 1)
                dve.wait_ge(rstd_done, norm_no(n, t))

            dve.wait_ge(rel_done, 1)
            nc.vector.tensor_copy(rel_row[:, 0:SEQ], bank[0:N_MOBA, 0, :]).then_inc(rel_copied, 1)
            nc.vector.tensor_copy(rel_row[:, SEQ:REL], bank[0:N_MOBA, 1, 0:REL - SEQ]).then_inc(rel_copied, 1)
            for t in range(TT):
                inverse_std(SQ1, t)
                nc.vector.tensor_scalar(xn[:, t, :], x_sb[:, t, :], rstd[:, SQ1, t:t + 1], None,
                                        ALU.mult).then_inc(xn_done, 1)
            split(0)
            dve.wait_ge(small_in, 64)
            for k in range(KT):
                dve.wait_ge(hn_hi_done, k + 1)
                nc.vector.scalar_tensor_tensor(out=hn_lo[:, k, :], in0=bank[:, 2 + k % 6, :],
                                               scalar=g_mix_c[:, k:k + 1], in1=hn_hi[:, k, :], op0=ALU.mult,
                                               op1=ALU.subtract).then_inc(hn_lo_done, 1)
            split(1)
            split(2)
            dve.wait_ge(wf_hi_done, 1)
            nc.vector.tensor_tensor(wf_lo[:, :, :], wf_raw[:, :, :], wf_hi[:, :, :], ALU.subtract
                                    ).then_inc(wf_lo_done, 1)
            split(3)

            def conv_tail(G):
                c, m = divmod(G - CONV_GROUP, 3)
                src = bank[:, PROJ[G % 2], :]
                dve.wait_ge(proj_done, G + 1)
                if m == 0:
                    dve.wait_ge(s_done, 8 * (PAIRS - 1))
                    nc.vector.memset(conv_u[:, 0:2], 0.0).then_inc(conv_step, 1)
                    nc.vector.tensor_copy(conv_c[:, :], src).then_inc(proj_read, 1)
                elif m == 1:
                    dve.wait_ge(proj_read, G)
                    dve.wait_ge(conv_step, 4 * c + 1)
                    nc.vector.tensor_tensor(conv_u[:, 2:2 + SEQ], src, conv_c[:, :], ALU.mult
                                            ).then_inc(proj_read, 1)
                    dve.wait_ge(proj_read, G + 1)
                    nc.vector.tensor_scalar(conv_y[:, :], conv_u[:, 2:2 + SEQ], conv_w_c[:, c, 2:3], None,
                                            ALU.mult).then_inc(conv_step, 1)
                    for n, tap in enumerate((1, 0)):
                        dve.wait_ge(conv_step, 4 * c + 2 + n)
                        nc.vector.scalar_tensor_tensor(out=conv_y[:, :], in0=conv_u[:, tap:tap + SEQ],
                                                       scalar=conv_w_c[:, c, tap:tap + 1], in1=conv_y[:, :],
                                                       op0=ALU.mult, op1=ALU.add).then_inc(conv_step, 1)
                else:
                    dve.wait_ge(conv_step, 4 * c + 4)
                    if c > 0:
                        dve.wait_ge(conv_lo, c)
                    nc.vector.tensor_tensor(conv_o[:, :], src, conv_y[:, :], ALU.mult).then_inc(proj_read, 1)

            def evac_lo(G):
                if G >= CONV_GROUP:
                    conv_tail(G)
                    return
                p, j = (0, G) if G < 3 else ((G - 4) // 3 + 1, (G - 4) % 3)
                src = bank[:, PROJ[G % 2], :]
                if G == F_GROUP:
                    dve.wait_ge(proj_done, G + 1)
                    nc.vector.tensor_scalar(f_z[:, :], src[0:N_FOX, :], bf_c[:, :], None, ALU.add
                                            ).then_inc(proj_read, 1)
                    dve.wait_ge(proj_read, G + 1)
                    nc.vector.tensor_scalar(f_abs[:, :], f_z[:, :], -1.0, None, ALU.mult).then_inc(f_z_done, 1)
                    dve.wait_ge(f_z_done, 1)
                    nc.vector.tensor_tensor(f_abs[:, :], f_z[:, :], f_abs[:, :], ALU.max).then_inc(f_z_done, 1)
                    dve.wait_ge(f_log_done, 2)
                    nc.vector.scalar_tensor_tensor(out=f_z[:, :], in0=f_z[:, :], scalar=0.0, in1=f_log[:, :],
                                                   op0=ALU.min, op1=ALU.subtract).then_inc(f_z_done, 1)
                    dve.wait_ge(f_z_done, 3)
                    dve.wait_ge(consts_done, 8)
                    nc.vector.tensor_tensor_scan(f_cum[:, :], f_one[:, :], f_z[:, :], 0.0, ALU.mult,
                                                 ALU.subtract).then_inc(f_cum_done, 1)
                elif j == 2:
                    dve.wait_ge(proj_done, G + 1)
                    if p >= 1:
                        dve.wait_ge(vT_done, p)
                    else:
                        dve.wait_ge(sq_done, TT)
                    nc.vector.tensor_copy(vT[:, :], src).then_inc(proj_read, 1)
                else:
                    dst = (q_hl, k_hl)[j][p % 2]
                    dve.wait_ge(proj_hi, 2 * p + j + 1)
                    for h in range(2):
                        last = nc.vector.scalar_tensor_tensor(
                            out=dst[DH:P, h, :], in0=src[DH * h:DH * (h + 1), :], scalar=SCALE if j == 0 else 1.0,
                            in1=dst[0:DH, h, :], op0=ALU.mult, op1=ALU.subtract)
                    last.then_inc(proj_read, 1)

            def evac_v(p):
                dve.wait_ge(v_hi_done, p + 1)
                nc.vector.tensor_tensor(v_lo[p % 2][:, :, 0:3:2, :],
                                        bank[:, VTBANK, :].rearrange("p (j h d) -> p j h d", j=TT, h=2),
                                        v_hi[p % 2][:, :, 0:3:2, :], ALU.subtract).then_inc(v_lo_done, 1)

            def evac_pT(g):
                i = g % 4
                dve.wait_ge(pT_hi_done, g + 1)
                nc.vector.tensor_tensor(pT_lo[:, 0:i + 1, P * i:P * (i + 1)],
                                        bank[:, TBANK[g % 2], 0:P * (i + 1)].rearrange("p (j q) -> p j q", q=P),
                                        pT_hi[:, 0:i + 1, P * i:P * (i + 1)], ALU.subtract).then_inc(pT_lo_done, 1)

            def evac_o(p):
                dve.wait_ge(o_hi, p + 1)
                nc.vector.tensor_tensor(cat_lo[:, p, :], bank[:, OBANK, :], cat_hi[:, p, :], ALU.subtract
                                        ).then_inc(o_lo, 1)

            for G in range(F_GROUP + 1):
                evac_lo(G)

            conv_lo_at = {5: 0, 8: 1}
            for g in range(STEPS + 2):
                p, s = divmod(g, 8)
                if g < STEPS:
                    i, h = g % 4, (g // 4) % 2
                    n = P * (i + 1)
                    dve.wait_ge(s_done, g + 1)
                    if s == 0:
                        dve.wait_ge(bias_in[p % 2], 32 * (p // 2 + 1))
                    if g >= 2:
                        dve.wait_ge(exp_done, g - 1)
                    bias_ap = bias[:, p % 2, h, 0:n]
                    if p < MOBA_PAIRS:
                        bias_ap = bias_ap[:, ::-1]
                    nc.vector.tensor_tensor_reduce(
                        out=logits[:, g % 2, 0:n], in0=bank[:, SBANK[g % 2], 0:n], in1=bias_ap,
                        scale=-1.0, scalar=3.0e38, op0=ALU.add, op1=ALU.min,
                        accum_out=neg_max[:, g:g + 1]).then_inc(biased, 1)
                if g >= 1:
                    for G in finished(g - 1):
                        evac_lo(G)
                for u in splits_at(g):
                    split(u)
                if p < PAIRS and s == 2:
                    evac_v(p)
                if g < STEPS:
                    dve.wait_ge(exp_done, g + 1)
                    nc.vector.reciprocal(row_inv[:, g:g + 1], row_sum[:, g:g + 1]).then_inc(inv_done, 1)
                    dve.wait_ge(inv_done, g + 1)
                    nc.vector.tensor_scalar(probs[:, g % 2, 0:n], probs[:, g % 2, 0:n], row_inv[:, g:g + 1], None,
                                            ALU.mult).then_inc(normed, 1)
                if 1 <= g <= STEPS:
                    evac_pT(g - 1)
                if g >= 9 and (g - 9) % 8 == 1:
                    evac_o((g - 9) // 8)
                if g - 8 * (PAIRS - 1) in conv_lo_at:
                    c = conv_lo_at[g - 8 * (PAIRS - 1)]
                    dve.wait_ge(conv_hi, c + 1)
                    nc.vector.tensor_tensor(cat_lo[:, 6 + c, :], conv_o[:, :], cat_hi[:, 6 + c, :], ALU.subtract
                                            ).then_inc(conv_lo, 1)
            split(U_WOUT + 4)
            split(U_WOUT + 5)
            evac_o(PAIRS - 1)
            for u in range(U_WOUT + 6, U_GU + 2):
                split(u)

            def evac_h2(t):
                for b in range(2):
                    dve.wait_ge(h2_hi, 2 * t + b + 1)
                    nc.vector.tensor_tensor(hn_lo[:, 4 * b:4 * b + 4, P * t:P * (t + 1)],
                                            bank[:, TBANK[b], :].rearrange("p (k q) -> p k q", q=P),
                                            hn_hi[:, 4 * b:4 * b + 4, P * t:P * (t + 1)], ALU.subtract
                                            ).then_inc(h2_lo, 1)

            for t in range(TT):
                if t == TT - 1:
                    split(U_GU + 2)
                    split(U_GU + 3)
                if t >= 1:
                    evac_h2(t - 1)
                if t == 0:
                    dve.wait_ge(g_mix_in, 32)
                inverse_std(SQ2, t)
                b = 2 * (t % 2)
                y = mix_y[:, t % 2, :]
                if t >= 2:
                    dve.wait_ge(h2T_done, 2 * (t - 1))
                nc.vector.scalar_tensor_tensor(out=y, in0=bank[:, b:b + 2, :].rearrange("p a n -> p (a n)"),
                                               scalar=rstd[:, SQ2, t:t + 1], in1=g_post_mix_b[:, :], op0=ALU.mult,
                                               op1=ALU.mult).then_inc(mix_normed, 1)
                dve.wait_ge(mix_normed, t + 1)
                nc.vector.tensor_tensor(x_sb[:, t, :], x_sb[:, t, :], y, ALU.add).then_inc(x1_done, 1)
                inverse_std(SQ3, t)
                nc.vector.scalar_tensor_tensor(out=y, in0=x_sb[:, t, :], scalar=rstd[:, SQ3, t:t + 1],
                                               in1=g_pre_ffn_b[:, :], op0=ALU.mult, op1=ALU.mult
                                               ).then_inc(h2_done, 1)
            evac_h2(TT - 1)

            def gated(f, par):
                dve.wait_ge(silu_done, f + 1)
                dve.wait_ge(up_done, f + 1)
                dst = act[:, f, :] if isinstance(f, int) else \
                    act[:, bass.ds(f, 1), :].rearrange("p o n -> p (o n)")
                nc.vector.tensor_tensor(dst, bank[:, GU_BANKS[par][1], :], silu_g[:, par, :], ALU.mult
                                        ).then_inc(act_done, 1)
                for n in range(2):
                    split(U_GU + 4 + 2 * par + n, f * 2 + (U_GU + 4 + n + 1))

            for f in range(2):
                gated(f, f)
            with dve.Fori(1, FT // 2) as i:
                for par in range(2):
                    gated(i * 2 + par, par)

            def act_split(f, n, count):
                hi = act_hi[:, n, :] if n < 2 else lact_hi[:, n - 2, :]
                lo = act_lo[:, n, :] if n < 2 else lact_lo[:, n - 2, :]
                src = act[:, f, :] if isinstance(f, int) else act[:, bass.ds(f, 1), :].rearrange("p o n -> p (o n)")
                dve.wait_ge(act_hi_done, count)
                nc.vector.tensor_tensor(lo, src, hi, ALU.subtract).then_inc(act_lo_done, 1)

            dve.wait_ge(act_done, FT)
            act_split(0, 0, 1)
            act_split(1, 1, 2)
            with dve.Fori(0, LOOP_DOWN // 4 - 1) as i:
                for j in range(4):
                    split(U_DOWN + 4 + j, i * 4 + (U_DOWN + 4 + j + 1))
                    act_split(i * 4 + (j + 2), j % 2, i * 4 + (j + 3))
            for n in range(2):
                f = LOOP_DOWN - 2 + n
                act_split(f, n, f + 1)
                split(U_DOWN + LOOP_DOWN + n)
            for n in range(LAST):
                act_split(LOOP_DOWN + n, 2 + n, LOOP_DOWN + n + 1)
                if n + 2 < LAST:
                    split(U_DOWN + LOOP_DOWN + n + 2)

            dve.wait_ge(g_ffn_in, 16)
            dve.wait_ge(act_lo_done, FT)
            for t in range(TT):
                inverse_std(SQ4, t)
                b = DOWN_BANKS[t]
                nc.vector.scalar_tensor_tensor(out=ff_y[:, t, :], in0=bank[:, b:b + 2, :].rearrange("p a n -> p (a n)"),
                                               scalar=rstd[:, SQ4, t:t + 1], in1=g_post_ffn_b[:, :], op0=ALU.mult,
                                               op1=ALU.mult).then_inc(ff_normed, 1)
                dve.wait_ge(ff_normed, t + 1)
                nc.vector.tensor_tensor(ff_y[:, t, :], ff_y[:, t, :], x_sb[:, t, :], ALU.add).then_inc(y_done, 1)

        @block.tensor
        def _(pe):
            def product(out_ap, st, mv, first, last, check=False):
                (sh, sl), (mh, ml) = st, mv
                nc.tensor.matmul(out_ap, sh, mh, start=first, stop=False, skip_group_check=check)
                nc.tensor.matmul(out_ap, sh, ml, start=False, stop=False, skip_group_check=check)
                return nc.tensor.matmul(out_ap, sl, mh, start=False, stop=last, skip_group_check=check)

            pe.wait_ge(tables_in, 32)
            nc.tensor.matmul(bank[0:N_MOBA, 0, :], relb[:, :], onehot[:, 0:SEQ], start=True, stop=True)
            nc.tensor.matmul(bank[0:N_MOBA, 1, 0:REL - SEQ], relb[:, :], onehot[:, SEQ:REL], start=True, stop=True
                             ).then_inc(rel_done, 1)

            pe.wait_ge(consts_done, 5)
            for t in range(TT):
                pe.wait_ge(xn_done, t + 1)
                for k in range(6):
                    mm = nc.tensor.transpose(bank[:, 2 + k, P * t:P * (t + 1)], xn[:, t, P * k:P * (k + 1)],
                                             ident[:, :])
                    if t == TT - 1:
                        mm.then_inc(xT_done, 1)
            for k in range(6, KT):
                pe.wait_ge(hn_lo_done, k - 5)
                for t in range(TT):
                    mm = nc.tensor.transpose(bank[:, 2 + k % 6, P * t:P * (t + 1)], xn[:, t, P * k:P * (k + 1)],
                                             ident[:, :])
                mm.then_inc(xT_done, 1)

            def proj_step(G, u, k):
                if k == 0:
                    pe.wait_ge(lo_done, u + 1)
                    if G >= 2:
                        pe.wait_ge(proj_read, G - 1)
                hi, lo = w_hi[u % 4], w_lo[u % 4]
                mm = product(bank[:, PROJ[G % 2], :], (hi[:, k, :], lo[:, k, :]), (hn_hi[:, k, :], hn_lo[:, k, :]),
                             k == 0, k == KT - 1)
                if k == KT - 1:
                    mm.then_inc(proj_done, 1)

            pe.wait_ge(rel_copied, 2)
            for j in range(3):
                for k in range(KT):
                    if j == 0:
                        pe.wait_ge(hn_lo_done, k + 1)
                    proj_step(group(0, j), j, k)
            pe.wait_ge(wf_lo_done, 1)
            pe.wait_ge(proj_read, F_GROUP - 1)
            for k in range(KT):
                mm = product(bank[0:P, PROJ[F_GROUP % 2], :][0:N_FOX], (wf_hi[:, k, :], wf_lo[:, k, :]),
                             (hn_hi[:, k, :], hn_lo[:, k, :]), k == 0, k == KT - 1)
            mm.then_inc(proj_done, 1)

            def logits_step(g):
                p, s = divmod(g, 8)
                h, i = divmod(s, 4)
                n = P * (i + 1)
                if s == 0:
                    pe.wait_ge(proj_read, group(p, 1) + 1)
                    pe.wait_ge(swapped, 4 * p + 4)
                if g >= 2:
                    pe.wait_ge(biased, g - 1)
                b = SBANK[g % 2]
                q = slice(P * i, P * (i + 1))
                k_ap = k_hl[p % 2][:, h, 0:n]
                nc.tensor.matmul(bank[:, b, 0:n], q_hl[p % 2][:, h, q], k_ap, start=True, stop=False,
                                 skip_group_check=True)
                nc.tensor.matmul(bank[:, b, 0:n], q_lh[p % 2][:, h, q], k_ap, start=False, stop=False,
                                 skip_group_check=True)
                nc.tensor.matmul(bank[:, b, P * i:n], ident_b[:, :], mask_b[:, :], start=False, stop=True,
                                 skip_group_check=True).then_inc(s_done, 1)

            def transpose_step(g):
                i = g % 4
                pe.wait_ge(normed, g + 1)
                if g >= 2:
                    pe.wait_ge(pT_lo_done, g - 1)
                for j in range(i + 1):
                    mm = nc.tensor.transpose(bank[:, TBANK[g % 2], P * j:P * (j + 1)],
                                             probs[:, g % 2, P * j:P * (j + 1)], ident[:, :])
                mm.then_inc(t_done, 1)

            def pv(head):
                p, h = divmod(head, 2)
                pe.wait_ge(pT_lo_done, 4 * head + 4)
                pe.wait_ge(v_lo_done, p + 1)
                if h == 0 and p >= 1:
                    pe.wait_ge(o_lo, p)
                for j in range(TT):
                    vh = v_hi[p % 2][:, j, h:h + 2, :].rearrange("p a d -> p (a d)")
                    vl = v_lo[p % 2][:, j, h:h + 2, :].rearrange("p a d -> p (a d)")
                    mm = product(bank[:, OBANK, P * j:SEQ], (vh, vl),
                                 (pT_hi[:, j, P * j:SEQ], pT_lo[:, j, P * j:SEQ]),
                                 h == 0 and j == 0, h == 1 and j == TT - 1, check=True)
                mm.then_inc(pv_done, 1)

            def v_tokens(p):
                pe.wait_ge(proj_read, group(p, 2) + 1)
                if p >= 1:
                    pe.wait_ge(v_lo_done, p)
                for j in range(TT):
                    mm = nc.tensor.transpose(bank[:, VTBANK, P * j:P * (j + 1)], vT[:, P * j:P * (j + 1)],
                                             ident[:, :])
                mm.then_inc(vT_done, 1)

            def mix_part(t, n):
                k = WOUT_ORDER[n]
                if t == 0:
                    pe.wait_ge(lo_done, U_WOUT + n + 1)
                    if k < PAIRS:
                        pe.wait_ge(o_lo, k + 1)
                    else:
                        pe.wait_ge(conv_lo, k - PAIRS + 1)
                hi, lo = split_slot(U_WOUT + n)
                for h in range(2):
                    c = slice(4 * h, 4 * h + 4)
                    mm = product(bank[:, 2 * (t % 2) + h, :],
                                 (cat_hi[:, k, P * t:P * (t + 1)], cat_lo[:, k, P * t:P * (t + 1)]),
                                 (hi[:, c, :].rearrange("p k n -> p (k n)"), lo[:, c, :].rearrange("p k n -> p (k n)")),
                                 n == 0, n == KT - 1)
                if t == TT - 1 and n < 7:
                    mm.then_inc(mix_unit_used, 1)
                if n == KT - 1:
                    mm.then_inc(mix_done, 1)

            for g in range(STEPS + 1):
                p, s = divmod(g, 8)
                if g < STEPS:
                    logits_step(g)
                if p < PAIRS - 1:
                    for n in range(3 * s, 3 * s + 3):
                        proj_step(group(p + 1, n // 8), 3 * (p + 1) + n // 8, n % 8)
                elif g < STEPS:
                    for n in range(6 * s, 6 * s + 6):
                        proj_step(CONV_GROUP + n // 8, 3 * PAIRS + n // 8, n % 8)
                if g >= 5 and (g - 1) % 4 == 0:
                    pv((g - 5) // 4)
                if g >= 1:
                    transpose_step(g - 1)
                if p < PAIRS and s == 1:
                    v_tokens(p)

            pe.wait_ge(proj_read, GROUPS)
            for n in range(4):
                mix_part(0, n)
            pv(2 * PAIRS - 1)
            for n in range(4, KT):
                mix_part(0, n)

            def h2_tokens(t):
                pe.wait_ge(h2_done, t + 1)
                for b in range(2):
                    if t >= 1:
                        pe.wait_ge(h2_lo, 2 * t - 1 + b)
                    else:
                        pe.wait_ge(pT_lo_done, STEPS)
                    for k in range(4 * b, 4 * b + 4):
                        mm = nc.tensor.transpose(bank[:, TBANK[b], P * (k % 4):P * (k % 4 + 1)],
                                                 mix_y[:, t % 2, P * k:P * (k + 1)], ident[:, :])
                    mm.then_inc(h2T_done, 1)

            for t in range(1, TT):
                if t >= 2:
                    pe.wait_ge(mix_normed, t - 1)
                for n in range(KT):
                    mix_part(t, n)
                    if n == 6:
                        h2_tokens(t - 1)

            def gate_up(slots, par, tokens, count):
                for w, (b, slot, done) in enumerate(zip(GU_BANKS[par], slots, (gate_done, up_done))):
                    for k in range(KT):
                        mm = product(bank[:, b, tokens], (slot[0][:, k, :], slot[1][:, k, :]),
                                     (hn_hi[:, k, tokens], hn_lo[:, k, tokens]), k == 0, k == KT - 1)
                    if count:
                        mm.then_inc(done, 1)

            pe.wait_ge(lo_done, U_GU + 2)
            pe.wait_ge(h2_lo, 2 * (TT - 1))
            pe.wait_ge(o_lo, PAIRS)
            pe.wait_ge(v_lo_done, PAIRS)
            first = [split_slot(U_GU), split_slot(U_GU + 1)]
            gate_up(first, 0, slice(0, SEQ - P), False)
            h2_tokens(TT - 1)
            pe.wait_ge(h2_lo, 2 * TT)
            gate_up(first, 0, slice(SEQ - P, SEQ), True)
            pe.wait_ge(lo_done, U_GU + 4)
            gate_up([(w_hi[2], w_lo[2]), (w_hi[3], w_lo[3])], 1, slice(0, SEQ), True)
            with pe.Fori(1, FT // 2) as i:
                for par in range(2):
                    pe.wait_ge(lo_done, i * 4 + (U_GU + 2 * par + 2))
                    pe.wait_ge(act_done, i * 2 + (par - 1))
                    s = 2 * par
                    gate_up([(w_hi[s], w_lo[s]), (w_hi[s + 1], w_lo[s + 1])], par, slice(0, SEQ), True)

            def down(units, acts, t, first, last):
                for h in range(2):
                    c = slice(4 * h, 4 * h + 4)
                    mm = product(bank[:, DOWN_BANKS[t] + h, :],
                                 (acts[0][:, P * t:P * (t + 1)], acts[1][:, P * t:P * (t + 1)]),
                                 (units[0][:, c, :].rearrange("p k n -> p (k n)"),
                                  units[1][:, c, :].rearrange("p k n -> p (k n)")), first, last)
                return mm

            pe.wait_ge(mix_normed, TT)
            pe.wait_ge(act_done, FT)

            def down_turn(j, count, first):
                pe.wait_ge(act_lo_done, count)
                for t in range(TT):
                    mm = down((w_hi[j], w_lo[j]), (act_hi[:, j % 2, :], act_lo[:, j % 2, :]), t, first, False)
                mm.then_inc(down_done, 1)

            for j in range(4):
                down_turn(j, j + 1, j == 0)
            with pe.Fori(1, LOOP_DOWN // 4) as i:
                for j in range(4):
                    pe.wait_ge(lo_done, i * 4 + (U_DOWN + j + 1))
                    down_turn(j, i * 4 + (j + 1), False)
            for t in range(TT):
                for n in range(LAST):
                    if t == 0:
                        pe.wait_ge(lo_done, U_DOWN + LOOP_DOWN + n + 1)
                        pe.wait_ge(act_lo_done, LOOP_DOWN + n + 1)
                    mm = down((last_hi[n], last_lo[n]), (lact_hi[:, n, :], lact_lo[:, n, :]), t, False,
                              n == LAST - 1)
                mm.then_inc(down_tile, 1)


def bucket_table():
    import math
    import numpy as np
    dist = np.maximum(np.arange(REL) - (P - 1), 0)
    exact = BUCKETS // 2
    far = np.log(np.maximum(dist, 1).astype(np.float32) / np.float32(exact)) / np.float32(math.log(128 / exact))
    large = np.minimum(exact + (far * np.float32(BUCKETS - exact)).astype(np.int32), BUCKETS - 1)
    bucket = np.where(dist < exact, dist, large)
    return (np.arange(BUCKETS)[:, None] == bucket[None, :]).astype(np.float32)


def kernel(x, w_in, b_f, conv_w, w_out, rel_bias, g_pre_mix, g_post_mix, g_pre_ffn, g_post_ffn, w_gate, w_up,
           w_down):
    import numpy as np
    import concourse.bacc as bacc
    from concourse.bass_utils import run_bass_kernel_spmd

    def units(w):
        w = np.asarray(w)
        n = w.shape[1] // P
        return np.ascontiguousarray(w.reshape(KT, P, n, P).transpose(2, 1, 0, 3).reshape(n, P, KT * P))

    w = np.asarray(w_in)[0]
    fox0 = 3 * MOBA_W
    conv0 = fox0 + 3 * FOX_W + N_FOX
    starts = [base + P * p + j * MOBA_W for base in (0, fox0) for p in range(MOBA_PAIRS) for j in range(3)]
    starts += [conv0 + P * c + CONV_CH * m for c in range(2) for m in (1, 2, 0)]
    tiles = np.concatenate([w[:, s:s + P] for s in starts], axis=1)
    w_f = w[:, fox0 + 3 * FOX_W:conv0].reshape(KT, P, N_FOX).transpose(1, 0, 2)
    arrays = {
        "x": np.asarray(x)[0],
        "w_in_units": units(tiles),
        "w_f": w_f,
        "b_f": np.asarray(b_f).reshape(N_FOX, 1),
        "conv_w": np.asarray(conv_w)[0].reshape(3, 2, P).transpose(2, 1, 0),
        "w_out": np.asarray(w_out)[0],
        "rel_bias": np.asarray(rel_bias),
        "bucket_onehot": bucket_table(),
        "g_pre_mix": np.asarray(g_pre_mix).reshape(KT, P).T,
        "g_post_mix": np.asarray(g_post_mix).reshape(D),
        "g_pre_ffn": np.asarray(g_pre_ffn).reshape(D),
        "g_post_ffn": np.asarray(g_post_ffn).reshape(D),
        "w_gate_units": units(np.asarray(w_gate)[0]),
        "w_up_units": units(np.asarray(w_up)[0]),
        "w_down": np.asarray(w_down)[0],
    }
    nc = bacc.Bacc("TRN2", target_bir_lowering=False, num_devices=1)
    ins, args = {}, []
    for name, a in arrays.items():
        a = np.ascontiguousarray(a)
        ins[f"in_{name}"] = a
        args.append(nc.dram_tensor(f"in_{name}", a.shape, mybir.dt.from_np(a.dtype), kind="ExternalInput").ap())
    out = nc.dram_tensor("out", (SEQ, D), F32, kind="ExternalOutput").ap()
    hybrid_block(nc, *args, out)
    r = run_bass_kernel_spmd(nc, [ins], core_ids=[0])
    return r.results[0]["out"].reshape(1, SEQ, D)
```

```python
from contextlib import ExitStack

import concourse.bass as bass
from concourse import mybir

ALU = mybir.AluOpType
ACT = mybir.ActivationFunctionType
F32 = mybir.dt.float32
F32R = mybir.dt.float32r
BF16 = mybir.dt.bfloat16

P = 128
SEQ = 512
D = 1024
TT = SEQ // P
KT = D // P
DH = 64
N_MOBA = 6
N_FOX = 6
PAIRS = (N_MOBA + N_FOX) // 2
MOBA_PAIRS = N_MOBA // 2
CONV_CH = 256
D_FF = 2816
FT = D_FF // P
MOBA_W = N_MOBA * DH
FOX_W = N_FOX * DH
EPS = 1e-6
SCALE = DH ** -0.5
MASKED = -1.0e30
BUCKETS = 32
REL = 640

U_WOUT = 24
U_GU = U_WOUT + KT
U_DOWN = U_GU + 2 * FT
WOUT_ORDER = [6, 0, 1, 2, 3, 4, 7, 5]
RAW = 4
LOOP_DOWN = 16
LAST = FT - LOOP_DOWN

PROJ = (0, 1)
SBANK = (2, 3)
TBANK = (4, 5)
OBANK = 6
VTBANK = 7
MIX_BANKS = (2, 0, 2, 0)
GU_BANKS = ((6, 7), (2, 3))
DOWN_BANKS = (0, 4, 6, 2)

STEPS = 8 * PAIRS


def group(p, j):
    return j if p == 0 else 4 + 3 * (p - 1) + j


F_GROUP = 3
CONV_GROUP = group(PAIRS, 0)
GROUPS = CONV_GROUP + 6


WOUT_SLOT = (0, 1, "ext0", 2, 3, "ext1", "ext2", "ext3")


def unit_group(u):
    return group(u // 3, u % 3)


def slot_groups(u):
    if u < U_WOUT:
        return unit_group(u - 4) + 1
    slot = WOUT_SLOT[u - U_WOUT]
    return unit_group(U_WOUT - 4 + slot) + 1 if isinstance(slot, int) else 0


def has_hi(G):
    return G != F_GROUP and G < CONV_GROUP and (G if G < 3 else G - 4) % 3 != 2


def finished(g):
    if g < 0:
        return []
    p, s = divmod(g, 8)
    if p < PAIRS - 1:
        return [group(p + 1, j) for j in range(3) if (8 * j + 7) // 3 == s]
    if p == PAIRS - 1:
        return [CONV_GROUP + m for m in range(6) if (8 * m + 7) // 6 == s]
    return []


def splits_at(g):
    if g < 0:
        return []
    p, s = divmod(g, 8)
    if p < PAIRS - 1:
        return [u for at, u in ((0, 3 * p + 5), (4, 3 * p + 6), (5, 3 * p + 7)) if at == s]
    s = g - 8 * (PAIRS - 1)
    return [3 * PAIRS + 2 + n for n, at in enumerate((0, 1, 2, 3, 4, 6, 6, 7, 8)) if at == s]


def hybrid_block(nc, x, w_in_units, w_f, b_f, conv_w, w_out, rel_bias, bucket_onehot, g_pre_mix, g_post_mix,
                 g_pre_ffn, g_post_ffn, w_gate_units, w_up_units, w_down, out):
    rel_rows = nc.dram_tensor("rel_rows", (N_MOBA, REL), F32, kind="Internal")
    cum_rows = nc.dram_tensor("cum_rows", (N_FOX, SEQ), F32, kind="Internal")

    with ExitStack() as ctx:
        def sem(name):
            return ctx.enter_context(nc.semaphore(name))

        base = (nc.sbuf_base + 63) // 64 * 64
        KB = 1024

        def at(name, offset, shape, dt=F32):
            return nc.alloc_sbuf_tensor_at(name, shape, dt, offset=base + offset)

        o = 0
        x_sb = at("x_sb", o, [P, TT, D]); o += 16 * KB
        hn_hi = at("hn_hi", o, [P, KT, SEQ], F32R)
        hn_lo = at("hn_lo", o + 16 * KB, [P, KT, SEQ], F32R)
        last3 = o
        lact_hi = at("lact_hi", o + 8 * KB, [P, LAST, SEQ], F32R)
        lact_lo = at("lact_lo", o + 20 * KB, [P, LAST, SEQ], F32R); o += 32 * KB
        cat_hi = at("cat_hi", o, [P, KT, SEQ], F32R)
        cat_lo = at("cat_lo", o + 16 * KB, [P, KT, SEQ], F32R)
        last_at = [o, o + 8 * KB, o + 16 * KB, last3]
        last_hi = [at(f"last_hi{n}", last_at[n], [P, KT, P], F32R) for n in range(4)]
        last_lo = [at(f"last_lo{n}", last_at[n] + 4 * KB, [P, KT, P], F32R) for n in range(4)]
        act_hi = at("act_hi", o + 24 * KB, [P, 2, SEQ], F32R)
        act_lo = at("act_lo", o + 28 * KB, [P, 2, SEQ], F32R)
        o += 32 * KB
        raw = [at(f"raw{n}", o + 4 * KB * n, [P, KT, P]) for n in range(RAW)]; o += 4 * KB * RAW
        w_hi = [at(f"w_hi{n}", o + 8 * KB * n, [P, KT, P], F32R) for n in range(4)]
        w_lo = [at(f"w_lo{n}", o + 8 * KB * n + 4 * KB, [P, KT, P], F32R) for n in range(4)]; o += 32 * KB
        a = o
        v_hi, v_lo = [None] * 2, [None] * 2
        v_hi[0] = at("v_hi0", a, [P, TT, 3, DH], F32R)
        v_lo[0] = at("v_lo0", a + 3 * KB, [P, TT, 3, DH], F32R)
        vT = at("vT", a + 6 * KB, [P, SEQ])
        logits = at("logits", a + 8 * KB, [P, 2, SEQ])
        probs = at("probs", a + 12 * KB, [P, 2, SEQ])
        pT_hi = at("pT_hi", a + 16 * KB, [P, TT, SEQ], F32R)
        pT_lo = at("pT_lo", a + 24 * KB, [P, TT, SEQ], F32R)
        xn = at("xn", a + 16 * KB, [P, TT, D])
        squares = at("squares", a, [P, D])
        q_hl, q_lh, k_hl = [None] * 2, [None] * 2, [None] * 2
        for s in range(2):
            q_hl[s] = at(f"q_hl{s}", a + (32 + 12 * s) * KB, [P, 2, SEQ], F32R)
            q_lh[s] = at(f"q_lh{s}", a + (36 + 12 * s) * KB, [P, 2, SEQ], F32R)
            k_hl[s] = at(f"k_hl{s}", a + (40 + 12 * s) * KB, [P, 2, SEQ], F32R)
        conv_c = at("conv_c", a + 32 * KB, [P, SEQ])
        conv_y = at("conv_y", a + 34 * KB, [P, SEQ])
        conv_o = at("conv_o", a + 36 * KB, [P, SEQ])
        conv_u = at("conv_u", a + 38 * KB, [P, 2 + SEQ])
        v_hi[1] = at("v_hi1", a + 56 * KB, [P, TT, 3, DH], F32R)
        v_lo[1] = at("v_lo1", a + 59 * KB, [P, TT, 3, DH], F32R)
        bias = at("bias", a + 62 * KB, [P, 2, 2, SEQ])
        ext_hi = [at(f"ext_hi{n}", a + 8 * KB * n, [P, KT, P], F32R) for n in range(4)]
        ext_lo = [at(f"ext_lo{n}", a + 8 * KB * n + 4 * KB, [P, KT, P], F32R) for n in range(4)]
        fst_hi = [at(f"fst_hi{n}", a + (32 + 8 * n) * KB, [P, KT, P], F32R) for n in range(2)]
        fst_lo = [at(f"fst_lo{n}", a + (36 + 8 * n) * KB, [P, KT, P], F32R) for n in range(2)]
        mix_y = at("mix_y", a + 48 * KB, [P, 2, D])
        g_post_mix_b = at("g_post_mix_b", a + 56 * KB, [P, D])
        g_pre_ffn_b = at("g_pre_ffn_b", a + 60 * KB, [P, D])
        mix_sq = at("mix_sq", a + 64 * KB, [P, D])
        act = at("act", a, [P, FT, SEQ])
        silu_g = at("silu_g", a + 44 * KB, [P, 2, SEQ])
        for n in range(2):
            last_hi.append(at(f"last_hi{4 + n}", a + (48 + 8 * n) * KB, [P, KT, P], F32R))
            last_lo.append(at(f"last_lo{4 + n}", a + (52 + 8 * n) * KB, [P, KT, P], F32R))
        g_post_ffn_b = at("g_post_ffn_b", a + 64 * KB, [P, D])
        ff_y = at("ff_y", a, [P, TT, D])
        ff_sq = at("ff_sq", a + 16 * KB, [P, D])
        o = a + 70 * KB
        ident = at("ident", o, [P, P]); o += 512
        ident_b = at("ident_b", o, [P, P], BF16); o += 256
        mask_b = at("mask_b", o, [P, P], BF16); o += 256
        g_mix_c = at("g_mix_c", o, [P, KT]); o += 32
        conv_w_c = at("conv_w_c", o, [P, 2, 3]); o += 32
        wf_raw = at("wf_raw", o, [P, KT, N_FOX]); o += 192
        wf_hi = at("wf_hi", o, [P, KT, N_FOX], F32R); o += 192
        wf_lo = at("wf_lo", o, [P, KT, N_FOX], F32R); o += 192
        eps = at("eps", o, [P, 1]); o += 32
        bf_c = at("bf_c", o, [N_FOX, 1]); o += 32
        relb = at("relb", o, [BUCKETS + 1, N_MOBA]); o += 32
        sumsq = at("sumsq", o, [P, 4, TT]); o += 64
        half_sum = at("half_sum", o, [P, 2]); o += 32
        half_eps = at("half_eps", o, [P, 1]); o += 32
        std = at("std", o, [P, 4, TT]); o += 64
        rstd = at("rstd", o, [P, 4, TT]); o += 64
        neg_max = at("neg_max", o, [P, STEPS]); o += 192
        row_sum = at("row_sum", o, [P, STEPS]); o += 192
        row_inv = at("row_inv", o, [P, STEPS]); o += 192
        assert base + o <= nc.sbuf_usable_end, (base + o, nc.sbuf_usable_end)
        onehot = at("onehot", a + 62 * KB, [BUCKETS + 1, REL])
        rel_row = at("rel_row", a + 65 * KB, [N_MOBA, REL])
        f_one = at("f_one", 56 * KB, [N_FOX, SEQ])
        f_log = at("f_log", 58 * KB, [N_FOX, SEQ])
        f_abs = at("f_abs", 70 * KB, [N_FOX, SEQ])
        f_z = at("f_z", 72 * KB, [N_FOX, SEQ])
        f_cum = at("f_cum", 74 * KB, [N_FOX, SEQ])

        bank = ctx.enter_context(nc.psum_tensor("bank", [P, 8, SEQ], F32))

        x_in = [sem(f"x_in{t}") for t in range(TT)]
        tables_in = sem("tables_in")
        small_in = sem("small_in")
        wf_in = sem("wf_in")
        raw_in = [sem(f"raw_in{n}") for n in range(RAW)]
        bias_in = [sem(f"bias_in{n}") for n in range(2)]
        rel_out = sem("rel_out")
        cum_out = sem("cum_out")
        g_mix_in = sem("g_mix_in")
        g_ffn_in = sem("g_ffn_in")
        out_done = sem("out_done")
        consts_done = sem("consts_done")
        after_set = sem("after_set")
        rel_done = sem("rel_done")
        rel_copied = sem("rel_copied")
        sq_done = sem("sq_done")
        std_done = sem("std_done")
        rstd_done = sem("rstd_done")
        xn_done = sem("xn_done")
        xT_done = sem("xT_done")
        hn_hi_done = sem("hn_hi_done")
        hn_lo_done = sem("hn_lo_done")
        hi_done = sem("hi_done")
        lo_done = sem("lo_done")
        wf_hi_done = sem("wf_hi_done")
        wf_lo_done = sem("wf_lo_done")
        proj_done = sem("proj_done")
        proj_hi = sem("proj_hi")
        proj_read = sem("proj_read")
        swapped = [sem(f"swapped{n}") for n in range(2)]
        vT_done = sem("vT_done")
        v_hi_done = sem("v_hi_done")
        v_lo_done = sem("v_lo_done")
        f_z_done = sem("f_z_done")
        f_log_done = sem("f_log_done")
        f_cum_done = sem("f_cum_done")
        s_done = sem("s_done")
        biased = sem("biased")
        exp_done = sem("exp_done")
        inv_done = sem("inv_done")
        normed = sem("normed")
        t_done = sem("t_done")
        pT_hi_done = sem("pT_hi_done")
        pT_lo_done = sem("pT_lo_done")
        pv_done = sem("pv_done")
        o_hi = sem("o_hi")
        o_lo = sem("o_lo")
        conv_step = sem("conv_step")
        conv_hi = sem("conv_hi")
        conv_lo = sem("conv_lo")
        mix_unit_used = sem("mix_unit_used")
        mix_done = sem("mix_done")
        mix_normed = sem("mix_normed")
        x1_done = sem("x1_done")
        h2_done = sem("h2_done")
        h2T_done = sem("h2T_done")
        h2_hi = sem("h2_hi")
        h2_lo = sem("h2_lo")
        gate_done = sem("gate_done")
        up_done = sem("up_done")
        silu_done = sem("silu_done")
        act_done = sem("act_done")
        act_hi_done = sem("act_hi_done")
        act_lo_done = sem("act_lo_done")
        down_done = sem("down_done")
        down_tile = sem("down_tile")
        half_eps_done = sem("half_eps_done")
        half_scaled = sem("half_scaled")
        ff_normed = sem("ff_normed")
        y_done = sem("y_done")

        SQ1, SQ2, SQ3, SQ4 = range(4)

        def norm_no(n, t):
            return {SQ1: t + 1, SQ2: TT + 2 * t + 1, SQ3: TT + 2 * t + 2, SQ4: 3 * TT + t + 1}[n]

        def split_slot(u):
            if U_WOUT <= u < U_GU:
                slot = WOUT_SLOT[u - U_WOUT]
                if isinstance(slot, int):
                    return w_hi[slot], w_lo[slot]
                return ext_hi[int(slot[3])], ext_lo[int(slot[3])]
            if U_GU <= u < U_GU + 2:
                return fst_hi[u - U_GU], fst_lo[u - U_GU]
            if u >= U_DOWN + LOOP_DOWN:
                return last_hi[u - U_DOWN - LOOP_DOWN], last_lo[u - U_DOWN - LOOP_DOWN]
            return w_hi[u % 4], w_lo[u % 4]

        block = ctx.enter_context(nc.Block())

        @block.sync
        def _(sp):
            def load(u, src, free_value=None):
                if free_value is not None:
                    sp.wait_ge(lo_done, free_value)
                sp.dma_start(raw[u % RAW][:, :, :], src).then_inc(raw_in[u % RAW], 16)

            def unit(w, n):
                return w[n].rearrange("p (k n) -> p k n", n=P)

            def rows(w, k):
                return w[P * k:P * (k + 1), :].rearrange("p (k n) -> p k n", n=P)

            for t in range(TT):
                sp.dma_start(x_sb[:, t, :], x[P * t:P * (t + 1), :]).then_inc(x_in[t], 16)
            load(0, unit(w_in_units, 0))
            sp.dma_start(g_mix_c[:, :], g_pre_mix).then_inc(small_in, 16)
            sp.dma_start(bf_c[:, :], b_f).then_inc(small_in, 16)
            sp.dma_start(conv_w_c[:, :, :], conv_w).then_inc(small_in, 16)
            load(1, unit(w_in_units, 1))
            load(2, unit(w_in_units, 2))
            sp.dma_start(relb[0:BUCKETS, :], rel_bias).then_inc(tables_in, 16)
            sp.dma_start(onehot[:, :], bucket_onehot).then_inc(tables_in, 16)
            sp.dma_start(wf_raw[:, :, :], w_f).then_inc(wf_in, 16)
            for u in range(3, U_WOUT):
                load(u, unit(w_in_units, u), u - RAW + 1 if u >= RAW else None)
            for n, k in enumerate(WOUT_ORDER):
                load(U_WOUT + n, rows(w_out, k), U_WOUT + n - RAW + 1)
            with sp.Fori(0, FT // 2) as i:
                for j in range(4):
                    w = (w_gate_units, w_up_units)[j % 2]
                    load(U_GU + j, w[bass.ds(i * 2 + j // 2, 1)].rearrange("o p (k n) -> (o p) k n", n=P),
                         i * 4 + (U_GU + j - RAW + 1))
            with sp.Fori(0, LOOP_DOWN // 4) as i:
                for j in range(4):
                    load(U_DOWN + j, w_down[bass.ds(i * (4 * P) + P * j, P), :].rearrange("p (k n) -> p k n", n=P),
                         i * 4 + (U_DOWN + j - RAW + 1))
            for f in range(LOOP_DOWN, FT):
                load(U_DOWN + f, rows(w_down, f), U_DOWN + f - RAW + 1)
            for t in range(TT - 1):
                sp.wait_ge(y_done, t + 1)
                sp.dma_start(out[P * t:P * (t + 1), :], ff_y[:, t, :]).then_inc(out_done, 16)
            for h in range(2):
                sp.wait_ge(y_done, TT + h)
                sp.dma_start(out[P * (TT - 1):SEQ, SEQ * h:SEQ * (h + 1)], ff_y[:, TT - 1, SEQ * h:SEQ * (h + 1)]
                             ).then_inc(out_done, 16)
            sp.wait_ge(out_done, 16 * (TT + 1))

        @block.gpsimd
        def _(pool):
            nc.gpsimd.memset(eps[:, :], EPS).then_inc(consts_done, 1)
            nc.gpsimd.memset(ident[:, :], 1.0).then_inc(consts_done, 1)
            nc.gpsimd.memset(ident_b[:, :], 1.0).then_inc(consts_done, 1)
            nc.gpsimd.memset(mask_b[:, :], 0.0).then_inc(consts_done, 1)
            pool.wait_ge(consts_done, 4)
            for m in (ident, ident_b):
                nc.gpsimd.affine_select(out=m[:, :], in_=m[:, :], compare_op=ALU.is_equal, fill=0.0, base=0,
                                        pattern=[[-1, P]], channel_multiplier=1).then_inc(consts_done, 1)
            nc.gpsimd.affine_select(out=mask_b[:, :], in_=mask_b[:, :], compare_op=ALU.is_ge, fill=MASKED, base=0,
                                    pattern=[[-1, P]], channel_multiplier=1).then_inc(consts_done, 1)
            nc.gpsimd.memset(f_one[:, :], 1.0).then_inc(consts_done, 1)
            pool.wait_ge(sq_done, TT)
            for m in (v_hi[0], v_lo[0], v_hi[1], v_lo[1]):
                nc.gpsimd.memset(m[:, :, 1, :].bitcast(F32), 0.0).then_inc(consts_done, 1)

            def swap(p):
                s = p % 2
                pool.wait_ge(proj_hi, 2 * p + 1)
                pool.dma_start(q_lh[s][DH:P, :, :], q_hl[s][0:DH, :, :]).then_inc(swapped[s], 16)
                pool.wait_ge(proj_read, group(p, 0) + 1)
                pool.dma_start(q_lh[s][0:DH, :, :], q_hl[s][DH:P, :, :]).then_inc(swapped[s], 16)

            def load_bias(p):
                s = p % 2
                if p == 0:
                    pool.wait_ge(rel_out, 16)
                if p == MOBA_PAIRS:
                    pool.wait_ge(cum_out, 16)
                if p >= 2:
                    pool.wait_ge(biased, 8 * (p - 1))
                for h in range(2):
                    if p < MOBA_PAIRS:
                        src = bass.AP(rel_rows, (2 * p + h) * REL, [[1, P], [1, SEQ]])
                    else:
                        src = bass.AP(cum_rows, (2 * (p - MOBA_PAIRS) + h) * SEQ, [[0, P], [1, SEQ]])
                    pool.dma_start(bias[:, s, h, :], src).then_inc(bias_in[s], 16)

            swap(0)
            pool.wait_ge(rel_copied, 2)
            pool.dma_start(rel_rows.ap(), rel_row[:, :]).then_inc(rel_out, 16)

            for p in range(PAIRS):
                load_bias(p)
                if p >= 1:
                    swap(p)
                if p == 1:
                    pool.wait_ge(f_cum_done, 1)
                    pool.dma_start(cum_rows.ap(), f_cum[:, :]).then_inc(cum_out, 16)

            pool.wait_ge(pv_done, 2 * PAIRS)
            pool.wait_ge(biased, STEPS)
            pool.dma_start(g_post_mix_b[:, :], g_post_mix.partition_broadcast(P)).then_inc(g_mix_in, 16)
            pool.dma_start(g_pre_ffn_b[:, :], g_pre_ffn.partition_broadcast(P)).then_inc(g_mix_in, 16)
            pool.wait_ge(sq_done, 3 * TT)
            pool.dma_start(g_post_ffn_b[:, :], g_post_ffn.partition_broadcast(P)).then_inc(g_ffn_in, 16)

        @block.scalar
        def _(act_e):
            def split(u, value=None):
                hi, _ = split_slot(u)
                v = u if value is None else value
                act_e.wait_ge(raw_in[u % RAW], 16 * (v // RAW + 1) if value is None else value)
                nc.scalar.copy(hi[:, :, :], raw[u % RAW][:, :, :]).then_inc(hi_done, 1)

            def sum_squares(n, t, src, junk):
                nc.scalar.activation(junk, src, ACT.Square, accum_out=sumsq[:, n, t:t + 1]).then_inc(sq_done, 1)
                act_e.wait_ge(sq_done, norm_no(n, t))
                nc.scalar.activation(std[:, n, t:t + 1], sumsq[:, n, t:t + 1], ACT.Sqrt, bias=eps[:, :],
                                     scale=1.0 / D).then_inc(std_done, 1)

            nc.scalar.preload_act_table(ACT.Sqrt)
            act_e.wait_ge(consts_done, 1)
            for t in range(TT):
                act_e.wait_ge(x_in[t], 16)
                sum_squares(SQ1, t, x_sb[:, t, :], squares[:, :])
            split(0)
            act_e.wait_ge(small_in, 48)
            for k in range(KT):
                act_e.wait_ge(xT_done, k + 1)
                nc.scalar.activation(hn_hi[:, k, :], bank[:, 2 + k % 6, :], ACT.Copy,
                                     scale=g_mix_c[:, k:k + 1]).then_inc(hn_hi_done, 1)
            split(1)
            split(2)
            act_e.wait_ge(wf_in, 16)
            nc.scalar.copy(wf_hi[:, :, :], wf_raw[:, :, :]).then_inc(wf_hi_done, 1)
            split(3)

            def evac_hi(G):
                if G == F_GROUP or G >= CONV_GROUP:
                    return
                p, j = (0, G) if G < 3 else ((G - 4) // 3 + 1, (G - 4) % 3)
                if j == 2:
                    return
                act_e.wait_ge(proj_done, G + 1)
                if p >= 2 and j == 0:
                    act_e.wait_ge(s_done, 8 * (p - 1))
                dst = (q_hl, k_hl)[j][p % 2]
                for h in range(2):
                    last = nc.scalar.activation(dst[0:DH, h, :], bank[DH * h:DH * (h + 1), PROJ[G % 2], :], ACT.Copy,
                                                scale=SCALE if j == 0 else 1.0)
                last.then_inc(proj_hi, 1)

            def evac_v(p):
                act_e.wait_ge(vT_done, p + 1)
                if p >= 2:
                    act_e.wait_ge(pv_done, 2 * (p - 1))
                nc.scalar.copy(v_hi[p % 2][:, :, 0:3:2, :],
                               bank[:, VTBANK, :].rearrange("p (j h d) -> p j h d", j=TT, h=2)).then_inc(v_hi_done, 1)

            def evac_pT(g):
                i = g % 4
                act_e.wait_ge(t_done, g + 1)
                if g >= 4:
                    act_e.wait_ge(pv_done, g // 4)
                nc.scalar.copy(pT_hi[:, 0:i + 1, P * i:P * (i + 1)],
                               bank[:, TBANK[g % 2], 0:P * (i + 1)].rearrange("p (j q) -> p j q", q=P)
                               ).then_inc(pT_hi_done, 1)

            def evac_o(p):
                act_e.wait_ge(pv_done, 2 * p + 2)
                nc.scalar.copy(cat_hi[:, p, :], bank[:, OBANK, :]).then_inc(o_hi, 1)

            def forget_log():
                act_e.wait_ge(f_z_done, 2)
                nc.scalar.activation(f_abs[:, :], f_abs[:, :], ACT.Exp, scale=-1.0).then_inc(f_log_done, 1)
                act_e.wait_ge(f_log_done, 1)
                nc.scalar.activation(f_log[:, :], f_abs[:, :], ACT.Ln, bias=1.0).then_inc(f_log_done, 1)

            evac_hi(group(0, 0))
            split(4)
            evac_hi(group(0, 1))

            nc.scalar.preload_act_table_set("natural_log_exp_and_others")
            conv_hi_at = {5: 0, 8: 1}
            for g in range(STEPS + 2):
                p, s = divmod(g, 8)
                if g < STEPS:
                    act_e.wait_ge(biased, g + 1)
                    if g >= 2:
                        act_e.wait_ge(t_done, g - 1)
                    n = P * (g % 4 + 1)
                    nc.scalar.activation(probs[:, g % 2, 0:n], logits[:, g % 2, 0:n], ACT.Exp, scale=-1.0,
                                         bias=neg_max[:, g:g + 1], accum_out=row_sum[:, g:g + 1]
                                         ).then_inc(exp_done, 1)
                for u in splits_at(g):
                    if slot_groups(u):
                        act_e.wait_ge(proj_done, slot_groups(u))
                    else:
                        act_e.wait_ge(pv_done, 2 * PAIRS - 2)
                        act_e.wait_ge(vT_done, PAIRS)
                    split(u)
                if g >= 1:
                    for G in finished(g - 1):
                        evac_hi(G)
                if p < PAIRS and s == 2:
                    evac_v(p)
                if g == 1:
                    forget_log()
                if 1 <= g <= STEPS:
                    evac_pT(g - 1)
                if g >= 9 and (g - 9) % 8 == 1:
                    evac_o((g - 9) // 8)
                if g - 8 * (PAIRS - 1) in conv_hi_at:
                    c = conv_hi_at[g - 8 * (PAIRS - 1)]
                    act_e.wait_ge(proj_read, CONV_GROUP + 3 * c + 3)
                    nc.scalar.copy(cat_hi[:, 6 + c, :], conv_o[:, :]).then_inc(conv_hi, 1)
            act_e.wait_ge(t_done, STEPS)
            split(U_WOUT + 5)
            evac_o(PAIRS - 1)
            split(U_WOUT + 6)
            split(U_WOUT + 7)
            split(U_GU)
            split(U_GU + 1)

            def evac_h2(t):
                for b in range(2):
                    act_e.wait_ge(h2T_done, 2 * t + b + 1)
                    nc.scalar.copy(hn_hi[:, 4 * b:4 * b + 4, P * t:P * (t + 1)],
                                   bank[:, TBANK[b], :].rearrange("p (k q) -> p k q", q=P)).then_inc(h2_hi, 1)

            for t in range(TT):
                if t == TT - 1:
                    for n in range(2):
                        act_e.wait_ge(mix_unit_used, 4 + n)
                        split(U_GU + 2 + n)
                if t >= 1:
                    evac_h2(t - 1)
                act_e.wait_ge(mix_done, t + 1)
                b = MIX_BANKS[t]
                sum_squares(SQ2, t, bank[:, b:b + 2, :].rearrange("p a n -> p (a n)"), mix_sq[:, :])
                act_e.wait_ge(x1_done, t + 1)
                sum_squares(SQ3, t, x_sb[:, t, :], mix_sq[:, :])
            evac_h2(TT - 1)

            def silu(f, par):
                act_e.wait_ge(gate_done, f + 1)
                if isinstance(f, int) and f == 0:
                    act_e.wait_ge(up_done, 1)
                if not isinstance(f, int) or f >= 2:
                    act_e.wait_ge(act_done, f - 1)
                nc.scalar.activation(silu_g[:, par, :], bank[:, GU_BANKS[par][0], :], ACT.Silu).then_inc(silu_done, 1)

            def split_gu(f, par):
                act_e.wait_ge(up_done, f + 1)
                for n in range(2):
                    u = U_GU + 4 + 2 * par + n
                    split(u, f * 8 + (16 * (u // RAW + 1) - 8 * par))

            def act_split(f, n):
                dst = act_hi[:, n, :] if n < 2 else lact_hi[:, n - 2, :]
                nc.scalar.copy(dst, act[:, f, :]).then_inc(act_hi_done, 1)

            for f in range(2):
                silu(f, f)
                split_gu(f, f)
            for f in range(2):
                act_e.wait_ge(act_done, f + 1)
                act_split(f, f)
            with act_e.Fori(1, FT // 2) as i:
                for par in range(2):
                    silu(i * 2 + par, par)
                    split_gu(i * 2 + par, par)

            act_e.wait_ge(act_done, FT)

            def down_turn(i, j):
                act_e.wait_ge(down_done, i * 4 + (j + 1))
                split(U_DOWN + 4 + j, i * 16 + 16 * ((U_DOWN + 4) // RAW + 1))
                if isinstance(i, int):
                    act_split(4 * i + j + 2, j % 2)
                else:
                    nc.scalar.copy(act_hi[:, j % 2, :], act[:, bass.ds(i * 4 + (j + 2), 1), :].rearrange(
                        "p o n -> p (o n)")).then_inc(act_hi_done, 1)

            with act_e.Fori(0, LOOP_DOWN // 4 - 1) as i:
                for j in range(4):
                    down_turn(i, j)
            for n in range(2):
                f = LOOP_DOWN - 4 + n
                act_e.wait_ge(down_done, f + 1)
                act_split(f + 2, n)
                split(U_DOWN + LOOP_DOWN + n)
            for n in range(LAST):
                act_split(LOOP_DOWN + n, 2 + n)
                if n + 2 < LAST:
                    split(U_DOWN + LOOP_DOWN + n + 2)

            for t in range(TT - 1):
                act_e.wait_ge(down_tile, t + 1)
                b = DOWN_BANKS[t]
                sum_squares(SQ4, t, bank[:, b:b + 2, :].rearrange("p a n -> p (a n)"), ff_sq[:, :])
            t, b = TT - 1, DOWN_BANKS[TT - 1]
            for h in range(2):
                act_e.wait_ge(down_tile, TT + h)
                nc.scalar.activation(ff_sq[:, 0:SEQ], bank[:, b + h, :], ACT.Square,
                                     accum_out=half_sum[:, h:h + 1]).then_inc(sq_done, 1)
                act_e.wait_ge(sq_done, norm_no(SQ4, t) + h)
                if h == 0:
                    nc.scalar.activation(half_eps[:, :], half_sum[:, 0:1], ACT.Identity, bias=eps[:, :],
                                         scale=1.0 / D).then_inc(half_eps_done, 1)
                    act_e.wait_ge(half_eps_done, 1)
            nc.scalar.activation(std[:, SQ4, t:t + 1], half_sum[:, 1:2], ACT.Sqrt, bias=half_eps[:, :],
                                 scale=1.0 / D).then_inc(std_done, 1)

        @block.vector
        def _(dve):
            def split(u, value=None):
                hi, lo = split_slot(u)
                dve.wait_ge(hi_done, u + 1 if value is None else value)
                nc.vector.tensor_tensor(lo[:, :, :], raw[u % RAW][:, :, :], hi[:, :, :],
                                        ALU.subtract).then_inc(lo_done, 1)

            def inverse_std(n, t):
                dve.wait_ge(std_done, norm_no(n, t))
                nc.vector.reciprocal(rstd[:, n, t:t + 1], std[:, n, t:t + 1]).then_inc(rstd_done, 1)
                dve.wait_ge(rstd_done, norm_no(n, t))

            nc.vector.memset(relb[BUCKETS:BUCKETS + 1, :], MASKED).then_inc(after_set, 1)
            for t in range(TT):
                inverse_std(SQ1, t)
                nc.vector.tensor_scalar(xn[:, t, :], x_sb[:, t, :], rstd[:, SQ1, t:t + 1], None,
                                        ALU.mult).then_inc(xn_done, 1)
            split(0)
            dve.wait_ge(small_in, 48)
            for k in range(KT):
                dve.wait_ge(hn_hi_done, k + 1)
                nc.vector.scalar_tensor_tensor(out=hn_lo[:, k, :], in0=bank[:, 2 + k % 6, :],
                                               scalar=g_mix_c[:, k:k + 1], in1=hn_hi[:, k, :], op0=ALU.mult,
                                               op1=ALU.subtract).then_inc(hn_lo_done, 1)
            split(1)
            split(2)
            dve.wait_ge(wf_hi_done, 1)
            nc.vector.tensor_tensor(wf_lo[:, :, :], wf_raw[:, :, :], wf_hi[:, :, :], ALU.subtract
                                    ).then_inc(wf_lo_done, 1)
            split(3)

            def conv_tail(G):
                c, m = divmod(G - CONV_GROUP, 3)
                src = bank[:, PROJ[G % 2], :]
                dve.wait_ge(proj_done, G + 1)
                if m == 0:
                    dve.wait_ge(s_done, 8 * (PAIRS - 1))
                    nc.vector.memset(conv_u[:, 0:2], 0.0).then_inc(conv_step, 1)
                    nc.vector.tensor_copy(conv_c[:, :], src).then_inc(proj_read, 1)
                elif m == 1:
                    dve.wait_ge(proj_read, G)
                    dve.wait_ge(conv_step, 4 * c + 1)
                    nc.vector.tensor_tensor(conv_u[:, 2:2 + SEQ], src, conv_c[:, :], ALU.mult
                                            ).then_inc(proj_read, 1)
                    dve.wait_ge(proj_read, G + 1)
                    nc.vector.tensor_scalar(conv_y[:, :], conv_u[:, 2:2 + SEQ], conv_w_c[:, c, 2:3], None,
                                            ALU.mult).then_inc(conv_step, 1)
                    for n, tap in enumerate((1, 0)):
                        dve.wait_ge(conv_step, 4 * c + 2 + n)
                        nc.vector.scalar_tensor_tensor(out=conv_y[:, :], in0=conv_u[:, tap:tap + SEQ],
                                                       scalar=conv_w_c[:, c, tap:tap + 1], in1=conv_y[:, :],
                                                       op0=ALU.mult, op1=ALU.add).then_inc(conv_step, 1)
                else:
                    dve.wait_ge(conv_step, 4 * c + 4)
                    if c > 0:
                        dve.wait_ge(conv_lo, c)
                    nc.vector.tensor_tensor(conv_o[:, :], src, conv_y[:, :], ALU.mult).then_inc(proj_read, 1)

            def evac_lo(G):
                if G >= CONV_GROUP:
                    conv_tail(G)
                    return
                p, j = (0, G) if G < 3 else ((G - 4) // 3 + 1, (G - 4) % 3)
                src = bank[:, PROJ[G % 2], :]
                if j == 2:
                    dve.wait_ge(proj_done, G + 1)
                    if p >= 1:
                        dve.wait_ge(vT_done, p)
                    else:
                        dve.wait_ge(sq_done, TT)
                    nc.vector.tensor_copy(vT[:, :], src).then_inc(proj_read, 1)
                else:
                    dst = (q_hl, k_hl)[j][p % 2]
                    dve.wait_ge(proj_hi, 2 * p + j + 1)
                    for h in range(2):
                        last = nc.vector.scalar_tensor_tensor(
                            out=dst[DH:P, h, :], in0=src[DH * h:DH * (h + 1), :], scalar=SCALE if j == 0 else 1.0,
                            in1=dst[0:DH, h, :], op0=ALU.mult, op1=ALU.subtract)
                    last.then_inc(proj_read, 1)

            def forget_z():
                dve.wait_ge(proj_done, F_GROUP + 1)
                nc.vector.tensor_scalar(f_z[:, :], bank[0:N_FOX, PROJ[F_GROUP % 2], :], bf_c[:, :], None, ALU.add
                                        ).then_inc(proj_read, 1)
                dve.wait_ge(proj_read, F_GROUP + 1)
                nc.vector.tensor_scalar(f_abs[:, :], f_z[:, :], -1.0, None, ALU.mult).then_inc(f_z_done, 1)
                dve.wait_ge(f_z_done, 1)
                nc.vector.tensor_tensor(f_abs[:, :], f_z[:, :], f_abs[:, :], ALU.max).then_inc(f_z_done, 1)

            def forget_cum():
                dve.wait_ge(f_log_done, 2)
                nc.vector.scalar_tensor_tensor(out=f_z[:, :], in0=f_z[:, :], scalar=0.0, in1=f_log[:, :],
                                               op0=ALU.min, op1=ALU.subtract).then_inc(f_z_done, 1)
                dve.wait_ge(f_z_done, 3)
                dve.wait_ge(consts_done, 8)
                nc.vector.tensor_tensor_scan(f_cum[:, :], f_one[:, :], f_z[:, :], 0.0, ALU.mult,
                                             ALU.subtract).then_inc(f_cum_done, 1)

            def evac_v(p):
                dve.wait_ge(v_hi_done, p + 1)
                nc.vector.tensor_tensor(v_lo[p % 2][:, :, 0:3:2, :],
                                        bank[:, VTBANK, :].rearrange("p (j h d) -> p j h d", j=TT, h=2),
                                        v_hi[p % 2][:, :, 0:3:2, :], ALU.subtract).then_inc(v_lo_done, 1)

            def evac_pT(g):
                i = g % 4
                dve.wait_ge(pT_hi_done, g + 1)
                nc.vector.tensor_tensor(pT_lo[:, 0:i + 1, P * i:P * (i + 1)],
                                        bank[:, TBANK[g % 2], 0:P * (i + 1)].rearrange("p (j q) -> p j q", q=P),
                                        pT_hi[:, 0:i + 1, P * i:P * (i + 1)], ALU.subtract).then_inc(pT_lo_done, 1)

            def evac_o(p):
                dve.wait_ge(o_hi, p + 1)
                nc.vector.tensor_tensor(cat_lo[:, p, :], bank[:, OBANK, :], cat_hi[:, p, :], ALU.subtract
                                        ).then_inc(o_lo, 1)

            evac_lo(group(0, 0))
            evac_lo(group(0, 1))
            dve.wait_ge(rel_done, 1)
            nc.vector.tensor_copy(rel_row[:, 0:SEQ], bank[0:N_MOBA, OBANK, :]).then_inc(rel_copied, 1)
            nc.vector.tensor_copy(rel_row[:, SEQ:REL], bank[0:N_MOBA, VTBANK, 0:REL - SEQ]).then_inc(rel_copied, 1)
            evac_lo(group(0, 2))
            split(4)
            forget_z()

            conv_lo_at = {6: 0, 9: 1}
            for g in range(STEPS + 2):
                p, s = divmod(g, 8)
                for G in finished(g - 2):
                    if has_hi(G):
                        evac_lo(G)
                if g < STEPS:
                    i, h = g % 4, (g // 4) % 2
                    n = P * (i + 1)
                    dve.wait_ge(s_done, g + 1)
                    if s == 0:
                        dve.wait_ge(bias_in[p % 2], 32 * (p // 2 + 1))
                    if g >= 2:
                        dve.wait_ge(exp_done, g - 1)
                    bias_ap = bias[:, p % 2, h, 0:n]
                    if p < MOBA_PAIRS:
                        bias_ap = bias_ap[:, ::-1]
                    nc.vector.tensor_tensor_reduce(
                        out=logits[:, g % 2, 0:n], in0=bank[:, SBANK[g % 2], 0:n], in1=bias_ap,
                        scale=-1.0, scalar=3.0e38, op0=ALU.add, op1=ALU.min,
                        accum_out=neg_max[:, g:g + 1]).then_inc(biased, 1)
                for u in splits_at(g - 1):
                    split(u)
                for G in finished(g - 1):
                    if not has_hi(G):
                        evac_lo(G)
                if p < PAIRS and s == 3:
                    evac_v(p)
                if g == 5:
                    forget_cum()
                if g < STEPS:
                    dve.wait_ge(exp_done, g + 1)
                    nc.vector.reciprocal(row_inv[:, g:g + 1], row_sum[:, g:g + 1]).then_inc(inv_done, 1)
                    dve.wait_ge(inv_done, g + 1)
                    nc.vector.tensor_scalar(probs[:, g % 2, 0:n], probs[:, g % 2, 0:n], row_inv[:, g:g + 1], None,
                                            ALU.mult).then_inc(normed, 1)
                if 1 <= g <= STEPS:
                    evac_pT(g - 1)
                if g >= 9 and (g - 9) % 8 == 1:
                    evac_o((g - 9) // 8)
                if g - 8 * (PAIRS - 1) in conv_lo_at:
                    c = conv_lo_at[g - 8 * (PAIRS - 1)]
                    dve.wait_ge(conv_hi, c + 1)
                    nc.vector.tensor_tensor(cat_lo[:, 6 + c, :], conv_o[:, :], cat_hi[:, 6 + c, :], ALU.subtract
                                            ).then_inc(conv_lo, 1)
            split(U_WOUT + 5)
            evac_o(PAIRS - 1)
            split(U_WOUT + 6)
            split(U_WOUT + 7)
            dve.wait_ge(conv_lo, 2)
            split(U_GU)
            split(U_GU + 1)

            def evac_h2(t):
                for b in range(2):
                    dve.wait_ge(h2_hi, 2 * t + b + 1)
                    nc.vector.tensor_tensor(hn_lo[:, 4 * b:4 * b + 4, P * t:P * (t + 1)],
                                            bank[:, TBANK[b], :].rearrange("p (k q) -> p k q", q=P),
                                            hn_hi[:, 4 * b:4 * b + 4, P * t:P * (t + 1)], ALU.subtract
                                            ).then_inc(h2_lo, 1)

            for t in range(TT):
                if t == TT - 1:
                    split(U_GU + 2)
                    split(U_GU + 3)
                if t >= 1:
                    evac_h2(t - 1)
                if t == 0:
                    dve.wait_ge(g_mix_in, 32)
                inverse_std(SQ2, t)
                b = MIX_BANKS[t]
                y = mix_y[:, t % 2, :]
                if t >= 2:
                    dve.wait_ge(h2T_done, 2 * (t - 1))
                nc.vector.scalar_tensor_tensor(out=y, in0=bank[:, b:b + 2, :].rearrange("p a n -> p (a n)"),
                                               scalar=rstd[:, SQ2, t:t + 1], in1=g_post_mix_b[:, :], op0=ALU.mult,
                                               op1=ALU.mult).then_inc(mix_normed, 1)
                dve.wait_ge(mix_normed, t + 1)
                nc.vector.tensor_tensor(x_sb[:, t, :], x_sb[:, t, :], y, ALU.add).then_inc(x1_done, 1)
                inverse_std(SQ3, t)
                nc.vector.scalar_tensor_tensor(out=y, in0=x_sb[:, t, :], scalar=rstd[:, SQ3, t:t + 1],
                                               in1=g_pre_ffn_b[:, :], op0=ALU.mult, op1=ALU.mult
                                               ).then_inc(h2_done, 1)
            evac_h2(TT - 1)

            def gated(f, par):
                dve.wait_ge(silu_done, f + 1)
                dve.wait_ge(up_done, f + 1)
                dst = act[:, f, :] if isinstance(f, int) else \
                    act[:, bass.ds(f, 1), :].rearrange("p o n -> p (o n)")
                nc.vector.tensor_tensor(dst, bank[:, GU_BANKS[par][1], :], silu_g[:, par, :], ALU.mult
                                        ).then_inc(act_done, 1)
                for n in range(2):
                    split(U_GU + 4 + 2 * par + n, f * 2 + (U_GU + 4 + n + 1))

            def act_split(f, n, count):
                hi = act_hi[:, n, :] if n < 2 else lact_hi[:, n - 2, :]
                lo = act_lo[:, n, :] if n < 2 else lact_lo[:, n - 2, :]
                src = act[:, f, :] if isinstance(f, int) else act[:, bass.ds(f, 1), :].rearrange("p o n -> p (o n)")
                dve.wait_ge(act_hi_done, count)
                nc.vector.tensor_tensor(lo, src, hi, ALU.subtract).then_inc(act_lo_done, 1)

            for f in range(2):
                gated(f, f)
            for f in range(2):
                act_split(f, f, f + 1)
            with dve.Fori(1, FT // 2) as i:
                for par in range(2):
                    gated(i * 2 + par, par)
            dve.wait_ge(act_done, FT)
            with dve.Fori(0, LOOP_DOWN // 4 - 1) as i:
                for j in range(4):
                    split(U_DOWN + 4 + j, i * 4 + (U_DOWN + 4 + j + 1))
                    act_split(i * 4 + (j + 2), j % 2, i * 4 + (j + 3))
            for n in range(2):
                f = LOOP_DOWN - 2 + n
                act_split(f, n, f + 1)
                split(U_DOWN + LOOP_DOWN + n)
            for n in range(LAST):
                act_split(LOOP_DOWN + n, 2 + n, LOOP_DOWN + n + 1)
                if n + 2 < LAST:
                    split(U_DOWN + LOOP_DOWN + n + 2)

            dve.wait_ge(g_ffn_in, 16)
            dve.wait_ge(act_lo_done, FT)
            for t in range(TT - 1):
                inverse_std(SQ4, t)
                b = DOWN_BANKS[t]
                nc.vector.scalar_tensor_tensor(out=ff_y[:, t, :], in0=bank[:, b:b + 2, :].rearrange("p a n -> p (a n)"),
                                               scalar=rstd[:, SQ4, t:t + 1], in1=g_post_ffn_b[:, :], op0=ALU.mult,
                                               op1=ALU.mult).then_inc(ff_normed, 1)
                dve.wait_ge(ff_normed, t + 1)
                nc.vector.tensor_tensor(ff_y[:, t, :], ff_y[:, t, :], x_sb[:, t, :], ALU.add).then_inc(y_done, 1)
            t, b = TT - 1, DOWN_BANKS[TT - 1]
            halves = (slice(0, SEQ), slice(SEQ, D))
            for h, c in enumerate(halves):
                dve.wait_ge(sq_done, norm_no(SQ4, t) + h)
                nc.vector.tensor_tensor(ff_y[:, t, c], bank[:, b + h, :], g_post_ffn_b[:, c], ALU.mult
                                        ).then_inc(half_scaled, 1)
            inverse_std(SQ4, t)
            dve.wait_ge(half_scaled, 2)
            for c in halves:
                nc.vector.scalar_tensor_tensor(out=ff_y[:, t, c], in0=ff_y[:, t, c], scalar=rstd[:, SQ4, t:t + 1],
                                               in1=x_sb[:, t, c], op0=ALU.mult, op1=ALU.add).then_inc(y_done, 1)

        @block.tensor
        def _(pe):
            def product(out_ap, st, mv, first, last, check=False):
                (sh, sl), (mh, ml) = st, mv
                nc.tensor.matmul(out_ap, sh, mh, start=first, stop=False, skip_group_check=check)
                nc.tensor.matmul(out_ap, sh, ml, start=False, stop=False, skip_group_check=check)
                return nc.tensor.matmul(out_ap, sl, mh, start=False, stop=last, skip_group_check=check)

            pe.wait_ge(consts_done, 5)
            for t in range(TT):
                pe.wait_ge(xn_done, t + 1)
                for k in range(6):
                    mm = nc.tensor.transpose(bank[:, 2 + k, P * t:P * (t + 1)], xn[:, t, P * k:P * (k + 1)],
                                             ident[:, :])
                    if t == TT - 1:
                        mm.then_inc(xT_done, 1)
            for k in range(6, KT):
                pe.wait_ge(hn_lo_done, k - 5)
                for t in range(TT):
                    mm = nc.tensor.transpose(bank[:, 2 + k % 6, P * t:P * (t + 1)], xn[:, t, P * k:P * (k + 1)],
                                             ident[:, :])
                mm.then_inc(xT_done, 1)

            def proj_step(G, u, k):
                if k == 0:
                    pe.wait_ge(lo_done, u + 1)
                    if G >= 2:
                        pe.wait_ge(proj_read, G - 1)
                hi, lo = w_hi[u % 4], w_lo[u % 4]
                mm = product(bank[:, PROJ[G % 2], :], (hi[:, k, :], lo[:, k, :]), (hn_hi[:, k, :], hn_lo[:, k, :]),
                             k == 0, k == KT - 1)
                if k == KT - 1:
                    mm.then_inc(proj_done, 1)

            def relative_rows():
                pe.wait_ge(tables_in, 32)
                pe.wait_ge(after_set, 1)
                nc.tensor.matmul(bank[0:N_MOBA, OBANK, :], relb[:, :], onehot[:, 0:SEQ], start=True, stop=True)
                nc.tensor.matmul(bank[0:N_MOBA, VTBANK, 0:REL - SEQ], relb[:, :], onehot[:, SEQ:REL], start=True,
                                 stop=True).then_inc(rel_done, 1)

            for j in range(2):
                for k in range(KT):
                    if j == 0:
                        pe.wait_ge(hn_lo_done, k + 1)
                    proj_step(group(0, j), j, k)
            relative_rows()
            for k in range(KT):
                proj_step(group(0, 2), 2, k)
            pe.wait_ge(wf_lo_done, 1)
            pe.wait_ge(proj_read, F_GROUP - 1)
            for k in range(KT):
                mm = product(bank[0:P, PROJ[F_GROUP % 2], :][0:N_FOX], (wf_hi[:, k, :], wf_lo[:, k, :]),
                             (hn_hi[:, k, :], hn_lo[:, k, :]), k == 0, k == KT - 1)
            mm.then_inc(proj_done, 1)

            def logits_step(g):
                p, s = divmod(g, 8)
                h, i = divmod(s, 4)
                n = P * (i + 1)
                if s == 0:
                    pe.wait_ge(proj_read, group(p, 1) + 1)
                    pe.wait_ge(swapped[p % 2], 32 * (p // 2 + 1))
                if g >= 2:
                    pe.wait_ge(biased, g - 1)
                b = SBANK[g % 2]
                q = slice(P * i, P * (i + 1))
                k_ap = k_hl[p % 2][:, h, 0:n]
                nc.tensor.matmul(bank[:, b, 0:n], q_hl[p % 2][:, h, q], k_ap, start=True, stop=False,
                                 skip_group_check=True)
                mm = nc.tensor.matmul(bank[:, b, 0:n], q_lh[p % 2][:, h, q], k_ap, start=False,
                                      stop=p < MOBA_PAIRS, skip_group_check=True)
                if p < MOBA_PAIRS:
                    mm.then_inc(s_done, 1)
                    return
                nc.tensor.matmul(bank[:, b, P * i:n], ident_b[:, :], mask_b[:, :], start=False, stop=True,
                                 skip_group_check=True).then_inc(s_done, 1)

            def transpose_step(g):
                i = g % 4
                pe.wait_ge(normed, g + 1)
                if g >= 2:
                    pe.wait_ge(pT_lo_done, g - 1)
                for j in range(i + 1):
                    mm = nc.tensor.transpose(bank[:, TBANK[g % 2], P * j:P * (j + 1)],
                                             probs[:, g % 2, P * j:P * (j + 1)], ident[:, :])
                mm.then_inc(t_done, 1)

            def pv(head):
                p, h = divmod(head, 2)
                pe.wait_ge(pT_lo_done, 4 * head + 4)
                pe.wait_ge(v_lo_done, p + 1)
                if head == 0:
                    pe.wait_ge(consts_done, 12)
                if h == 0 and p >= 1:
                    pe.wait_ge(o_lo, p)
                for j in range(TT):
                    vh = v_hi[p % 2][:, j, h:h + 2, :].rearrange("p a d -> p (a d)")
                    vl = v_lo[p % 2][:, j, h:h + 2, :].rearrange("p a d -> p (a d)")
                    mm = product(bank[:, OBANK, P * j:SEQ], (vh, vl),
                                 (pT_hi[:, j, P * j:SEQ], pT_lo[:, j, P * j:SEQ]),
                                 h == 0 and j == 0, h == 1 and j == TT - 1, check=True)
                mm.then_inc(pv_done, 1)

            def v_tokens(p):
                pe.wait_ge(proj_read, group(p, 2) + 1)
                if p >= 1:
                    pe.wait_ge(v_lo_done, p)
                for j in range(TT):
                    mm = nc.tensor.transpose(bank[:, VTBANK, P * j:P * (j + 1)], vT[:, P * j:P * (j + 1)],
                                             ident[:, :])
                mm.then_inc(vT_done, 1)

            def mix_part(t, n):
                k = WOUT_ORDER[n]
                if t == 0:
                    pe.wait_ge(lo_done, U_WOUT + n + 1)
                    if k < PAIRS:
                        pe.wait_ge(o_lo, k + 1)
                    else:
                        pe.wait_ge(conv_lo, k - PAIRS + 1)
                hi, lo = split_slot(U_WOUT + n)
                for h in range(2):
                    c = slice(4 * h, 4 * h + 4)
                    mm = product(bank[:, MIX_BANKS[t] + h, :],
                                 (cat_hi[:, k, P * t:P * (t + 1)], cat_lo[:, k, P * t:P * (t + 1)]),
                                 (hi[:, c, :].rearrange("p k n -> p (k n)"), lo[:, c, :].rearrange("p k n -> p (k n)")),
                                 n == 0, n == KT - 1)
                if t == TT - 1 and n < 7:
                    mm.then_inc(mix_unit_used, 1)
                if n == KT - 1:
                    mm.then_inc(mix_done, 1)

            for g in range(STEPS):
                p, s = divmod(g, 8)
                logits_step(g)
                if p < PAIRS - 1:
                    for n in range(3 * s, 3 * s + 3):
                        proj_step(group(p + 1, n // 8), 3 * (p + 1) + n // 8, n % 8)
                else:
                    for n in range(6 * s, 6 * s + 6):
                        proj_step(CONV_GROUP + n // 8, 3 * PAIRS + n // 8, n % 8)
                if g >= 5 and (g - 1) % 4 == 0:
                    pv((g - 5) // 4)
                if 1 <= g < STEPS:
                    transpose_step(g - 1)
                if p < PAIRS and s == 1:
                    v_tokens(p)

            pe.wait_ge(biased, STEPS)
            for n in range(2):
                mix_part(0, n)
            transpose_step(STEPS - 1)
            for n in range(2, 4):
                mix_part(0, n)
            pv(2 * PAIRS - 1)
            for n in range(4, KT):
                mix_part(0, n)

            def h2_tokens(t):
                pe.wait_ge(h2_done, t + 1)
                for b in range(2):
                    if t >= 1:
                        pe.wait_ge(h2_lo, 2 * t - 1 + b)
                    else:
                        pe.wait_ge(pT_lo_done, STEPS)
                    for k in range(4 * b, 4 * b + 4):
                        mm = nc.tensor.transpose(bank[:, TBANK[b], P * (k % 4):P * (k % 4 + 1)],
                                                 mix_y[:, t % 2, P * k:P * (k + 1)], ident[:, :])
                    mm.then_inc(h2T_done, 1)

            for t in range(1, TT):
                if t == 1:
                    pe.wait_ge(proj_read, GROUPS)
                else:
                    pe.wait_ge(mix_normed, t - 1)
                for n in range(KT):
                    mix_part(t, n)
                    if n == (5 if t == TT - 1 else 6):
                        h2_tokens(t - 1)

            def ff_half(slot, b, tokens):
                for k in range(KT):
                    mm = product(bank[:, b, tokens], (slot[0][:, k, :], slot[1][:, k, :]),
                                 (hn_hi[:, k, tokens], hn_lo[:, k, tokens]), k == 0, k == KT - 1)
                return mm

            pe.wait_ge(lo_done, U_GU + 2)
            pe.wait_ge(h2_lo, 2 * (TT - 1))
            pe.wait_ge(o_lo, PAIRS)
            pe.wait_ge(v_lo_done, PAIRS)
            early, late, every = slice(0, SEQ - P), slice(SEQ - P, SEQ), slice(0, SEQ)
            g0, u0 = split_slot(U_GU), split_slot(U_GU + 1)
            g1, u1 = split_slot(U_GU + 2), split_slot(U_GU + 3)
            ff_half(g0, GU_BANKS[0][0], early)
            ff_half(u0, GU_BANKS[0][1], early)
            h2_tokens(TT - 1)
            pe.wait_ge(mix_normed, 3)
            pe.wait_ge(lo_done, U_GU + 3)
            ff_half(g1, GU_BANKS[1][0], early)
            pe.wait_ge(h2_lo, 2 * TT)
            ff_half(g0, GU_BANKS[0][0], late).then_inc(gate_done, 1)
            ff_half(u0, GU_BANKS[0][1], late).then_inc(up_done, 1)
            ff_half(g1, GU_BANKS[1][0], late).then_inc(gate_done, 1)
            pe.wait_ge(lo_done, U_GU + 4)
            ff_half(u1, GU_BANKS[1][1], every).then_inc(up_done, 1)
            with pe.Fori(1, FT // 2) as i:
                for par in range(2):
                    pe.wait_ge(lo_done, i * 4 + (U_GU + 2 * par + 2))
                    pe.wait_ge(act_done, i * 2 + (par - 1))
                    for n, done in enumerate((gate_done, up_done)):
                        s = 2 * par + n
                        ff_half((w_hi[s], w_lo[s]), GU_BANKS[par][n], every).then_inc(done, 1)

            def down(units, acts, t, first, last, halves=range(2)):
                for h in halves:
                    c = slice(4 * h, 4 * h + 4)
                    mm = product(bank[:, DOWN_BANKS[t] + h, :],
                                 (acts[0][:, P * t:P * (t + 1)], acts[1][:, P * t:P * (t + 1)]),
                                 (units[0][:, c, :].rearrange("p k n -> p (k n)"),
                                  units[1][:, c, :].rearrange("p k n -> p (k n)")), first, last)
                return mm

            pe.wait_ge(mix_normed, TT)

            def down_turn(j, count, first):
                pe.wait_ge(act_lo_done, count)
                for t in range(TT):
                    if first and t >= 2:
                        pe.wait_ge(act_done, FT - TT + 1 + t)
                    mm = down((w_hi[j], w_lo[j]), (act_hi[:, j % 2, :], act_lo[:, j % 2, :]), t, first, False)
                mm.then_inc(down_done, 1)

            for j in range(4):
                pe.wait_ge(lo_done, U_DOWN + j + 1)
                down_turn(j, j + 1, j == 0)
            with pe.Fori(1, LOOP_DOWN // 4) as i:
                for j in range(4):
                    pe.wait_ge(lo_done, i * 4 + (U_DOWN + j + 1))
                    down_turn(j, i * 4 + (j + 1), False)
            for t in range(TT):
                for halves in ((range(2),) if t < TT - 1 else ((0,), (1,))):
                    for n in range(LAST):
                        if t == 0:
                            pe.wait_ge(lo_done, U_DOWN + LOOP_DOWN + n + 1)
                            pe.wait_ge(act_lo_done, LOOP_DOWN + n + 1)
                        mm = down((last_hi[n], last_lo[n]), (lact_hi[:, n, :], lact_lo[:, n, :]), t, False,
                                  n == LAST - 1, halves)
                    mm.then_inc(down_tile, 1)


def bucket_table():
    import math
    import numpy as np
    dist = np.maximum(np.arange(REL) - (P - 1), 0)
    exact = BUCKETS // 2
    far = np.log(np.maximum(dist, 1).astype(np.float32) / np.float32(exact)) / np.float32(math.log(128 / exact))
    large = np.minimum(exact + (far * np.float32(BUCKETS - exact)).astype(np.int32), BUCKETS - 1)
    bucket = np.where(dist < exact, dist, large)
    bucket = np.where(np.arange(REL) < P - 1, BUCKETS, bucket)
    return (np.arange(BUCKETS + 1)[:, None] == bucket[None, :]).astype(np.float32)


def kernel(x, w_in, b_f, conv_w, w_out, rel_bias, g_pre_mix, g_post_mix, g_pre_ffn, g_post_ffn, w_gate, w_up,
           w_down):
    import numpy as np
    import concourse.bacc as bacc
    from concourse.bass_utils import run_bass_kernel_spmd

    def units(w):
        w = np.asarray(w)
        n = w.shape[1] // P
        return np.ascontiguousarray(w.reshape(KT, P, n, P).transpose(2, 1, 0, 3).reshape(n, P, KT * P))

    w = np.asarray(w_in)[0]
    fox0 = 3 * MOBA_W
    conv0 = fox0 + 3 * FOX_W + N_FOX
    starts = [base + P * p + j * MOBA_W for base in (0, fox0) for p in range(MOBA_PAIRS) for j in range(3)]
    starts += [conv0 + P * c + CONV_CH * m for c in range(2) for m in (1, 2, 0)]
    tiles = np.concatenate([w[:, s:s + P] for s in starts], axis=1)
    w_f = w[:, fox0 + 3 * FOX_W:conv0].reshape(KT, P, N_FOX).transpose(1, 0, 2)
    arrays = {
        "x": np.asarray(x)[0],
        "w_in_units": units(tiles),
        "w_f": w_f,
        "b_f": np.asarray(b_f).reshape(N_FOX, 1),
        "conv_w": np.asarray(conv_w)[0].reshape(3, 2, P).transpose(2, 1, 0),
        "w_out": np.asarray(w_out)[0],
        "rel_bias": np.asarray(rel_bias),
        "bucket_onehot": bucket_table(),
        "g_pre_mix": np.asarray(g_pre_mix).reshape(KT, P).T,
        "g_post_mix": np.asarray(g_post_mix).reshape(D),
        "g_pre_ffn": np.asarray(g_pre_ffn).reshape(D),
        "g_post_ffn": np.asarray(g_post_ffn).reshape(D),
        "w_gate_units": units(np.asarray(w_gate)[0]),
        "w_up_units": units(np.asarray(w_up)[0]),
        "w_down": np.asarray(w_down)[0],
    }
    nc = bacc.Bacc("TRN2", target_bir_lowering=False, num_devices=1)
    ins, args = {}, []
    for name, a in arrays.items():
        a = np.ascontiguousarray(a)
        ins[f"in_{name}"] = a
        args.append(nc.dram_tensor(f"in_{name}", a.shape, mybir.dt.from_np(a.dtype), kind="ExternalInput").ap())
    out = nc.dram_tensor("out", (SEQ, D), F32, kind="ExternalOutput").ap()
    hybrid_block(nc, *args, out)
    r = run_bass_kernel_spmd(nc, [ins], core_ids=[0])
    return r.results[0]["out"].reshape(1, SEQ, D)
```

```python
from contextlib import ExitStack

import concourse.bass as bass
from concourse import mybir

ALU = mybir.AluOpType
ACT = mybir.ActivationFunctionType
F32 = mybir.dt.float32
F32R = mybir.dt.float32r
BF16 = mybir.dt.bfloat16

P = 128
SEQ = 512
D = 1024
TT = SEQ // P
KT = D // P
DH = 64
N_MOBA = 6
N_FOX = 6
PAIRS = (N_MOBA + N_FOX) // 2
MOBA_PAIRS = N_MOBA // 2
CONV_CH = 256
D_FF = 2816
FT = D_FF // P
MOBA_W = N_MOBA * DH
FOX_W = N_FOX * DH
EPS = 1e-6
SCALE = DH ** -0.5
MASKED = -1.0e30
BUCKETS = 32
REL = 640
LO_COL = 32

U_WOUT = 24
U_GU = U_WOUT + KT
U_DOWN = U_GU + 2 * FT
WOUT_ORDER = [6, 0, 1, 2, 3, 4, 7, 5]
RAW = 4
LOOP_DOWN = 16
LAST = FT - LOOP_DOWN

PROJ = (0, 1)
SBANK = (2, 3)
TBANK = (4, 5)
OBANK = 6
VTBANK = 7
XT_BANKS = (2, 3, 4, 5, 6, 7, 2, 3)
MIX_BANKS = (2, 0, 2, 0)
GU_BANKS = ((6, 7), (2, 3))
DOWN_BANKS = (0, 4, 6, 2)

STEPS = 8 * PAIRS


def group(p, j):
    return j if p == 0 else 4 + 3 * (p - 1) + j


F_GROUP = 3
CONV_GROUP = group(PAIRS, 0)
GROUPS = CONV_GROUP + 6


WOUT_SLOT = ("ext0", 0, 1, 2, 3, "ext1", "ext2", "ext3")


def unit_group(u):
    return group(u // 3, u % 3)


def slot_groups(u):
    if u < U_WOUT:
        return unit_group(u - 4) + 1
    slot = WOUT_SLOT[u - U_WOUT]
    return unit_group(U_WOUT - 4 + slot) + 1 if isinstance(slot, int) else 0


def has_hi(G):
    return G != F_GROUP and G < CONV_GROUP and (G if G < 3 else G - 4) % 3 != 2


def finished(g):
    if g < 0:
        return []
    p, s = divmod(g, 8)
    if p < PAIRS - 1:
        return [group(p + 1, j) for j in range(3) if (8 * j + 7) // 3 == s]
    if p == PAIRS - 1:
        return [CONV_GROUP + m for m in range(6) if (8 * m + 7) // 6 == s]
    return []


def splits_at(g):
    if g < 0:
        return []
    p, s = divmod(g, 8)
    if p < PAIRS - 1:
        return [u for at, u in ((0, 3 * p + 5), (1, 3 * p + 6), (5, 3 * p + 7)) if at == s]
    return [3 * PAIRS + 2 + g - 8 * (PAIRS - 1)]


def hybrid_block(nc, x, w_in_units, w_f, b_f, conv_w, w_out, rel_bias, bucket_onehot, g_pre_mix, g_post_mix,
                 g_pre_ffn, g_post_ffn, w_gate_units, w_up_units, w_down, out):
    rel_rows = nc.dram_tensor("rel_rows", (N_MOBA, REL), F32, kind="Internal")
    cum_rows = nc.dram_tensor("cum_rows", (N_FOX, SEQ), F32, kind="Internal")

    with ExitStack() as ctx:
        def sem(name):
            return ctx.enter_context(nc.semaphore(name))

        base = (nc.sbuf_base + 63) // 64 * 64
        KB = 1024

        def at(name, offset, shape, dt=F32):
            return nc.alloc_sbuf_tensor_at(name, shape, dt, offset=base + offset)

        o = 0
        x_sb = at("x_sb", o, [P, TT, D]); o += 16 * KB
        hn_hi = at("hn_hi", o, [P, KT, SEQ], F32R)
        hn_lo = at("hn_lo", o + 16 * KB, [P, KT, SEQ], F32R)
        last3 = o
        lact_hi = at("lact_hi", o + 8 * KB, [P, LAST, SEQ], F32R)
        lact_lo = at("lact_lo", o + 20 * KB, [P, LAST, SEQ], F32R); o += 32 * KB
        cat_hi = at("cat_hi", o, [P, KT, SEQ], F32R)
        cat_lo = at("cat_lo", o + 16 * KB, [P, KT, SEQ], F32R)
        last_at = [o, o + 8 * KB, o + 16 * KB, last3]
        last_hi = [at(f"last_hi{n}", last_at[n], [P, KT, P], F32R) for n in range(4)]
        last_lo = [at(f"last_lo{n}", last_at[n] + 4 * KB, [P, KT, P], F32R) for n in range(4)]
        act_hi = at("act_hi", o + 24 * KB, [P, 2, SEQ], F32R)
        act_lo = at("act_lo", o + 28 * KB, [P, 2, SEQ], F32R)
        o += 32 * KB
        raw = [at(f"raw{n}", o + 4 * KB * n, [P, KT, P]) for n in range(RAW)]; o += 4 * KB * RAW
        w_hi = [at(f"w_hi{n}", o + 8 * KB * n, [P, KT, P], F32R) for n in range(4)]
        w_lo = [at(f"w_lo{n}", o + 8 * KB * n + 4 * KB, [P, KT, P], F32R) for n in range(4)]; o += 32 * KB
        a = o
        v_hl = [at("v_hl0", a, [P, TT, 2, P], F32R), at("v_hl1", a + 56 * KB, [P, TT, 2, P], F32R)]
        o_sum = at("o_sum", a + 60 * KB, [P, SEQ])
        vT = at("vT", a + 6 * KB, [P, SEQ])
        logits = at("logits", a + 8 * KB, [P, 2, SEQ])
        probs = [at("probs0", a + 12 * KB, [P, SEQ]), at("probs1", a + 14 * KB, [P, SEQ])]
        pT_hi = at("pT_hi", a + 16 * KB, [P, TT, SEQ], F32R)
        pT_lo = at("pT_lo", a + 24 * KB, [P, TT, SEQ], F32R)
        xn = at("xn", a + 16 * KB, [P, TT, D])
        squares = at("squares", a, [P, D])
        q_hl, q_lh, k_hl = [None] * 2, [None] * 2, [None] * 2
        for s in range(2):
            q_hl[s] = at(f"q_hl{s}", a + (32 + 12 * s) * KB, [P, 2, SEQ], F32R)
            q_lh[s] = at(f"q_lh{s}", a + (36 + 12 * s) * KB, [P, 2, SEQ], F32R)
            k_hl[s] = at(f"k_hl{s}", a + (40 + 12 * s) * KB, [P, 2, SEQ], F32R)
        conv_c = at("conv_c", a + 32 * KB, [P, SEQ])
        conv_y = at("conv_y", a + 34 * KB, [P, SEQ])
        conv_o = at("conv_o", a + 36 * KB, [P, SEQ])
        conv_u = at("conv_u", a + 38 * KB, [P, 2 + SEQ])
        bias = at("bias", a + 62 * KB, [P, 2, 2, SEQ])
        ext_at = [a, a + 8 * KB, a + 48 * KB, a + 40 * KB]
        ext_hi = [at(f"ext_hi{n}", ext_at[n], [P, KT, P], F32R) for n in range(4)]
        ext_lo = [at(f"ext_lo{n}", ext_at[n] + 4 * KB, [P, KT, P], F32R) for n in range(4)]
        fst_hi = [at(f"fst_hi{n}", a + (32 - 8 * n) * KB, [P, KT, P], F32R) for n in range(2)]
        fst_lo = [at(f"fst_lo{n}", a + (36 - 8 * n) * KB, [P, KT, P], F32R) for n in range(2)]
        mix_y = at("mix_y", a + 16 * KB, [P, 2, D])
        g_post_mix_b = at("g_post_mix_b", a + 56 * KB, [P, D])
        g_pre_ffn_b = at("g_pre_ffn_b", a + 60 * KB, [P, D])
        mix_sq = at("mix_sq", a + 64 * KB, [P, D])
        act = at("act", a, [P, FT, SEQ])
        silu_g = at("silu_g", a + 44 * KB, [P, 2, SEQ])
        for n in range(2):
            last_hi.append(at(f"last_hi{4 + n}", a + (48 + 8 * n) * KB, [P, KT, P], F32R))
            last_lo.append(at(f"last_lo{4 + n}", a + (52 + 8 * n) * KB, [P, KT, P], F32R))
        g_post_ffn_b = at("g_post_ffn_b", a + 64 * KB, [P, D])
        ff_y = at("ff_y", a, [P, TT, D])
        ff_sq = at("ff_sq", a + 16 * KB, [P, D])
        o = a + 70 * KB
        probs.append(at("probs2", o, [P, SEQ])); o += 2 * KB
        o_top = at("o_top", o, [DH, SEQ]); o += 2 * KB
        ident = at("ident", o, [P, P]); o += 512
        ident_b = at("ident_b", o, [P, P], BF16); o += 256
        mask_b = at("mask_b", o, [P, P], BF16); o += 256
        g_mix_c = at("g_mix_c", o, [P, KT]); o += 32
        conv_w_c = at("conv_w_c", o, [P, 2, 3]); o += 32
        wf_raw = at("wf_raw", o, [P, KT, N_FOX]); o += 192
        wf_hl = at("wf_hl", o, [P, KT, LO_COL + N_FOX], F32R); o += 1216
        eps = at("eps", o, [P, 1]); o += 32
        bf_c = at("bf_c", o, [N_FOX, 1]); o += 32
        relb = at("relb", o, [BUCKETS + 1, N_MOBA]); o += 32
        sumsq = at("sumsq", o, [P, 4, TT]); o += 64
        half_sum = at("half_sum", o, [P, 2]); o += 32
        half_eps = at("half_eps", o, [P, 1]); o += 32
        std = at("std", o, [P, 4, TT]); o += 64
        rstd = at("rstd", o, [P, 4, TT]); o += 64
        neg_max = at("neg_max", o, [P, STEPS]); o += 192
        row_sum = at("row_sum", o, [P, STEPS]); o += 192
        row_inv = at("row_inv", o, [P, STEPS]); o += 192
        assert base + o <= nc.sbuf_usable_end, (base + o, nc.sbuf_usable_end)
        onehot = at("onehot", a + 62 * KB, [BUCKETS + 1, REL])
        rel_row = at("rel_row", a + 65 * KB, [N_MOBA, REL])
        f_one = at("f_one", 56 * KB, [N_FOX, SEQ])
        f_log = at("f_log", 58 * KB, [N_FOX, SEQ])
        f_abs = at("f_abs", 70 * KB, [N_FOX, SEQ])
        f_z = at("f_z", 72 * KB, [N_FOX, SEQ])
        f_cum = at("f_cum", 74 * KB, [N_FOX, SEQ])

        bank = ctx.enter_context(nc.psum_tensor("bank", [P, 8, SEQ], F32))

        x_in = [sem(f"x_in{t}") for t in range(TT)]
        tables_in = sem("tables_in")
        small_in = sem("small_in")
        wf_in = sem("wf_in")
        raw_in = [sem(f"raw_in{n}") for n in range(RAW)]
        bias_in = [sem(f"bias_in{n}") for n in range(2)]
        rel_out = sem("rel_out")
        cum_out = sem("cum_out")
        g_post_mix_in = sem("g_post_mix_in")
        g_pre_ffn_in = sem("g_pre_ffn_in")
        g_ffn_in = sem("g_ffn_in")
        out_done = sem("out_done")
        consts_done = sem("consts_done")
        after_set = sem("after_set")
        rel_done = sem("rel_done")
        rel_copied = sem("rel_copied")
        sq_done = sem("sq_done")
        std_done = sem("std_done")
        rstd_done = sem("rstd_done")
        xn_done = sem("xn_done")
        xT_done = sem("xT_done")
        hn_hi_done = sem("hn_hi_done")
        hn_lo_done = sem("hn_lo_done")
        hi_done = sem("hi_done")
        lo_done = sem("lo_done")
        wf_hi_done = sem("wf_hi_done")
        wf_lo_done = sem("wf_lo_done")
        proj_done = sem("proj_done")
        proj_hi = sem("proj_hi")
        proj_read = sem("proj_read")
        swapped = [sem(f"swapped{n}") for n in range(2)]
        vT_done = sem("vT_done")
        v_hi_done = sem("v_hi_done")
        v_lo_done = sem("v_lo_done")
        f_z_part = sem("f_z_part")
        f_z_done = sem("f_z_done")
        f_log_done = sem("f_log_done")
        f_cum_done = sem("f_cum_done")
        s_done = sem("s_done")
        biased = sem("biased")
        exp_done = sem("exp_done")
        inv_done = sem("inv_done")
        normed = sem("normed")
        t_done = sem("t_done")
        pT_hi_done = sem("pT_hi_done")
        pT_lo_done = sem("pT_lo_done")
        pv_done = sem("pv_done")
        o_top_done = sem("o_top_done")
        o_summed = sem("o_summed")
        o_hi = sem("o_hi")
        o_lo = sem("o_lo")
        conv_step = sem("conv_step")
        conv_hi = sem("conv_hi")
        conv_lo = sem("conv_lo")
        mix_unit_used = sem("mix_unit_used")
        mix_done = sem("mix_done")
        mix_normed = sem("mix_normed")
        x1_done = sem("x1_done")
        h2_done = sem("h2_done")
        h2T_done = sem("h2T_done")
        h2_hi = sem("h2_hi")
        h2_lo = sem("h2_lo")
        gate_done = sem("gate_done")
        up_done = sem("up_done")
        silu_done = sem("silu_done")
        act_done = sem("act_done")
        act_hi_done = sem("act_hi_done")
        act_lo_done = sem("act_lo_done")
        down_done = sem("down_done")
        down_tile = sem("down_tile")
        half_eps_done = sem("half_eps_done")
        half_scaled = sem("half_scaled")
        ff_normed = sem("ff_normed")
        y_done = sem("y_done")

        SQ1, SQ2, SQ3, SQ4 = range(4)

        def norm_no(n, t):
            return {SQ1: t + 1, SQ2: TT + 2 * t + 1, SQ3: TT + 2 * t + 2, SQ4: 3 * TT + t + 1}[n]

        def split_slot(u):
            if U_WOUT <= u < U_GU:
                slot = WOUT_SLOT[u - U_WOUT]
                if isinstance(slot, int):
                    return w_hi[slot], w_lo[slot]
                return ext_hi[int(slot[3])], ext_lo[int(slot[3])]
            if U_GU <= u < U_GU + 2:
                return fst_hi[u - U_GU], fst_lo[u - U_GU]
            if u >= U_DOWN + LOOP_DOWN:
                return last_hi[u - U_DOWN - LOOP_DOWN], last_lo[u - U_DOWN - LOOP_DOWN]
            return w_hi[u % 4], w_lo[u % 4]

        block = ctx.enter_context(nc.Block())

        @block.sync
        def _(sp):
            def load(u, src, free_value=None):
                if free_value is not None:
                    sp.wait_ge(lo_done, free_value)
                sp.dma_start(raw[u % RAW][:, :, :], src).then_inc(raw_in[u % RAW], 16)

            def unit(w, n):
                return w[n].rearrange("p (k n) -> p k n", n=P)

            def rows(w, k):
                return w[P * k:P * (k + 1), :].rearrange("p (k n) -> p k n", n=P)

            for t in range(TT):
                sp.dma_start(x_sb[:, t, :], x[P * t:P * (t + 1), :]).then_inc(x_in[t], 16)
            load(0, unit(w_in_units, 0))
            sp.dma_start(g_mix_c[:, :], g_pre_mix).then_inc(small_in, 16)
            sp.dma_start(bf_c[:, :], b_f).then_inc(small_in, 16)
            sp.dma_start(conv_w_c[:, :, :], conv_w).then_inc(small_in, 16)
            load(1, unit(w_in_units, 1))
            load(2, unit(w_in_units, 2))
            sp.dma_start(relb[0:BUCKETS, :], rel_bias).then_inc(tables_in, 16)
            sp.dma_start(onehot[:, :], bucket_onehot).then_inc(tables_in, 16)
            sp.dma_start(wf_raw[:, :, :], w_f).then_inc(wf_in, 16)
            for u in range(3, U_WOUT):
                load(u, unit(w_in_units, u), u - RAW + 1 if u >= RAW else None)
            for n, k in enumerate(WOUT_ORDER):
                load(U_WOUT + n, rows(w_out, k), U_WOUT + n - RAW + 1)
            with sp.Fori(0, FT // 2) as i:
                for j in range(4):
                    w = (w_gate_units, w_up_units)[j % 2]
                    load(U_GU + j, w[bass.ds(i * 2 + j // 2, 1)].rearrange("o p (k n) -> (o p) k n", n=P),
                         i * 4 + (U_GU + j - RAW + 1))
            with sp.Fori(0, LOOP_DOWN // 4) as i:
                for j in range(4):
                    load(U_DOWN + j, w_down[bass.ds(i * (4 * P) + P * j, P), :].rearrange("p (k n) -> p k n", n=P),
                         i * 4 + (U_DOWN + j - RAW + 1))
            for f in range(LOOP_DOWN, FT):
                load(U_DOWN + f, rows(w_down, f), U_DOWN + f - RAW + 1)
            for t in range(TT - 1):
                sp.wait_ge(y_done, t + 1)
                sp.dma_start(out[P * t:P * (t + 1), :], ff_y[:, t, :]).then_inc(out_done, 16)
            for h in range(2):
                sp.wait_ge(y_done, TT + h)
                sp.dma_start(out[P * (TT - 1):SEQ, SEQ * h:SEQ * (h + 1)], ff_y[:, TT - 1, SEQ * h:SEQ * (h + 1)]
                             ).then_inc(out_done, 16)
            sp.wait_ge(out_done, 16 * (TT + 1))

        @block.gpsimd
        def _(pool):
            nc.gpsimd.memset(eps[:, :], EPS).then_inc(consts_done, 1)
            nc.gpsimd.memset(ident[:, :], 1.0).then_inc(consts_done, 1)
            nc.gpsimd.memset(ident_b[:, :], 1.0).then_inc(consts_done, 1)
            nc.gpsimd.memset(mask_b[:, :], 0.0).then_inc(consts_done, 1)
            pool.wait_ge(consts_done, 4)
            for m in (ident, ident_b):
                nc.gpsimd.affine_select(out=m[:, :], in_=m[:, :], compare_op=ALU.is_equal, fill=0.0, base=0,
                                        pattern=[[-1, P]], channel_multiplier=1).then_inc(consts_done, 1)
            nc.gpsimd.affine_select(out=mask_b[:, :], in_=mask_b[:, :], compare_op=ALU.is_ge, fill=MASKED, base=0,
                                    pattern=[[-1, P]], channel_multiplier=1).then_inc(consts_done, 1)
            nc.gpsimd.memset(wf_hl[:, :, :].bitcast(F32), 0.0).then_inc(consts_done, 1)
            nc.gpsimd.memset(f_one[:, :], 1.0).then_inc(consts_done, 1)

            def swap(p):
                s = p % 2
                pool.wait_ge(proj_hi, 2 * p + 1)
                pool.dma_start(q_lh[s][DH:P, :, :], q_hl[s][0:DH, :, :]).then_inc(swapped[s], 16)
                pool.wait_ge(proj_read, group(p, 0) + 1)
                pool.dma_start(q_lh[s][0:DH, :, :], q_hl[s][DH:P, :, :]).then_inc(swapped[s], 16)

            def load_bias(p):
                s = p % 2
                if p == 0:
                    pool.wait_ge(rel_out, 16)
                if p == MOBA_PAIRS:
                    pool.wait_ge(cum_out, 16)
                if p >= 2:
                    pool.wait_ge(biased, 8 * (p - 1))
                for h in range(2):
                    if p < MOBA_PAIRS:
                        src = bass.AP(rel_rows, (2 * p + h) * REL, [[1, P], [1, SEQ]])
                    else:
                        src = bass.AP(cum_rows, (2 * (p - MOBA_PAIRS) + h) * SEQ, [[0, P], [1, SEQ]])
                    pool.dma_start(bias[:, s, h, :], src).then_inc(bias_in[s], 16)

            swap(0)
            pool.wait_ge(rel_copied, 2)
            pool.dma_start(rel_rows.ap(), rel_row[:, :]).then_inc(rel_out, 16)

            for p in range(PAIRS):
                load_bias(p)
                if p >= 1:
                    swap(p)
                if p == 1:
                    pool.wait_ge(f_cum_done, 1)
                    pool.dma_start(cum_rows.ap(), f_cum[:, :]).then_inc(cum_out, 16)

            pool.wait_ge(pv_done, 2 * PAIRS)
            pool.wait_ge(biased, STEPS)
            pool.dma_start(g_post_mix_b[:, :], g_post_mix.partition_broadcast(P)).then_inc(g_post_mix_in, 16)
            pool.wait_ge(o_lo, PAIRS)
            pool.dma_start(g_pre_ffn_b[:, :], g_pre_ffn.partition_broadcast(P)).then_inc(g_pre_ffn_in, 16)
            pool.wait_ge(sq_done, 3 * TT)
            pool.dma_start(g_post_ffn_b[:, :], g_post_ffn.partition_broadcast(P)).then_inc(g_ffn_in, 16)

        @block.scalar
        def _(act_e):
            def split(u, value=None):
                hi, _ = split_slot(u)
                v = u if value is None else value
                act_e.wait_ge(raw_in[u % RAW], 16 * (v // RAW + 1) if value is None else value)
                nc.scalar.copy(hi[:, :, :], raw[u % RAW][:, :, :]).then_inc(hi_done, 1)

            def sum_squares(n, t, src, junk):
                nc.scalar.activation(junk, src, ACT.Square, accum_out=sumsq[:, n, t:t + 1]).then_inc(sq_done, 1)
                act_e.wait_ge(sq_done, norm_no(n, t))
                nc.scalar.activation(std[:, n, t:t + 1], sumsq[:, n, t:t + 1], ACT.Sqrt, bias=eps[:, :],
                                     scale=1.0 / D).then_inc(std_done, 1)

            nc.scalar.preload_act_table(ACT.Sqrt)
            act_e.wait_ge(consts_done, 1)
            for t in range(TT):
                act_e.wait_ge(x_in[t], 16)
                sum_squares(SQ1, t, x_sb[:, t, :], squares[:, :])
            split(0)
            act_e.wait_ge(small_in, 48)
            for k in range(KT):
                act_e.wait_ge(xT_done, k + 1)
                nc.scalar.activation(hn_hi[:, k, :], bank[:, XT_BANKS[k], :], ACT.Copy,
                                     scale=g_mix_c[:, k:k + 1]).then_inc(hn_hi_done, 1)
                if k == KT // 2 - 1:
                    split(1)
            split(2)
            act_e.wait_ge(wf_in, 16)
            act_e.wait_ge(consts_done, 8)
            nc.scalar.copy(wf_hl[:, :, 0:N_FOX], wf_raw[:, :, :]).then_inc(wf_hi_done, 1)
            split(3)

            def evac_hi(G):
                if G == F_GROUP or G >= CONV_GROUP:
                    return
                p, j = (0, G) if G < 3 else ((G - 4) // 3 + 1, (G - 4) % 3)
                if j == 2:
                    return
                act_e.wait_ge(proj_done, G + 1)
                if p >= 2 and j == 0:
                    act_e.wait_ge(s_done, 8 * (p - 1))
                dst = (q_hl, k_hl)[j][p % 2]
                for h in range(2):
                    last = nc.scalar.activation(dst[0:DH, h, :], bank[DH * h:DH * (h + 1), PROJ[G % 2], :], ACT.Copy,
                                                scale=SCALE if j == 0 else 1.0)
                last.then_inc(proj_hi, 1)

            def evac_v(p):
                act_e.wait_ge(vT_done, p + 1)
                if p >= 2:
                    act_e.wait_ge(pv_done, 2 * (p - 1))
                nc.scalar.copy(v_hl[p % 2][:, :, :, 0:DH],
                               bank[:, VTBANK, :].rearrange("p (j h d) -> p j h d", j=TT, h=2)).then_inc(v_hi_done, 1)

            def evac_pT(g):
                i = g % 4
                act_e.wait_ge(t_done, g + 1)
                if g >= 4:
                    act_e.wait_ge(pv_done, g // 4)
                nc.scalar.copy(pT_hi[:, 0:i + 1, P * i:P * (i + 1)],
                               bank[:, TBANK[g % 2], 0:P * (i + 1)].rearrange("p (j q) -> p j q", q=P)
                               ).then_inc(pT_hi_done, 1)

            def evac_o_top(head):
                act_e.wait_ge(pv_done, head + 1)
                if head >= 1:
                    act_e.wait_ge(o_summed, head)
                nc.scalar.copy(o_top[:, :], bank[DH:P, OBANK, :]).then_inc(o_top_done, 1)

            def evac_o(p):
                act_e.wait_ge(o_summed, 2 * p + 2)
                nc.scalar.copy(cat_hi[:, p, :], o_sum[:, :]).then_inc(o_hi, 1)

            def forget_log():
                act_e.wait_ge(f_z_done, 2)
                nc.scalar.activation(f_abs[:, :], f_abs[:, :], ACT.Exp, scale=-1.0).then_inc(f_log_done, 1)
                act_e.wait_ge(f_log_done, 1)
                nc.scalar.activation(f_log[:, :], f_abs[:, :], ACT.Ln, bias=1.0).then_inc(f_log_done, 1)

            evac_hi(group(0, 0))
            split(4)
            evac_hi(group(0, 1))

            nc.scalar.preload_act_table_set("natural_log_exp_and_others")
            conv_hi_at = {5: 0, 8: 1}
            for g in range(STEPS + 2):
                p, s = divmod(g, 8)
                if g < STEPS:
                    act_e.wait_ge(biased, g + 1)
                    if g >= 3:
                        act_e.wait_ge(t_done, g - 2)
                    n = P * (g % 4 + 1)
                    nc.scalar.activation(probs[g % 3][:, 0:n], logits[:, g % 2, 0:n], ACT.Exp, scale=-1.0,
                                         bias=neg_max[:, g:g + 1], accum_out=row_sum[:, g:g + 1]
                                         ).then_inc(exp_done, 1)
                if g >= 7 and g % 4 == 3:
                    evac_o_top((g - 7) // 4)
                for u in splits_at(g):
                    if slot_groups(u):
                        act_e.wait_ge(proj_done, slot_groups(u))
                    elif u == U_WOUT:
                        act_e.wait_ge(o_summed, 2 * PAIRS - 2)
                        act_e.wait_ge(vT_done, PAIRS)
                    else:
                        act_e.wait_ge(t_done, STEPS - 1)
                    split(u)
                if g >= 1:
                    for G in finished(g - 1):
                        evac_hi(G)
                if p < PAIRS and s == 2:
                    evac_v(p)
                if g == 1:
                    forget_log()
                if g >= 2:
                    evac_pT(g - 2)
                if g >= 12 and g % 8 == 4:
                    evac_o((g - 12) // 8)
                if g - 8 * (PAIRS - 1) in conv_hi_at:
                    c = conv_hi_at[g - 8 * (PAIRS - 1)]
                    act_e.wait_ge(proj_read, CONV_GROUP + 3 * c + 3)
                    nc.scalar.copy(cat_hi[:, 6 + c, :], conv_o[:, :]).then_inc(conv_hi, 1)
            split(U_WOUT + 6)
            act_e.wait_ge(conv_step, 8)
            split(U_WOUT + 7)
            evac_o_top(2 * PAIRS - 1)
            evac_o(PAIRS - 1)
            act_e.wait_ge(conv_lo, 2)
            split(U_GU)
            split(U_GU + 1)
            nc.scalar.preload_act_table(ACT.Sqrt)

            def evac_h2(t):
                for b in range(2):
                    act_e.wait_ge(h2T_done, 2 * t + b + 1)
                    nc.scalar.copy(hn_hi[:, 4 * b:4 * b + 4, P * t:P * (t + 1)],
                                   bank[:, TBANK[b], :].rearrange("p (k q) -> p k q", q=P)).then_inc(h2_hi, 1)

            for t in range(TT):
                if t == TT - 1:
                    for n in range(2):
                        act_e.wait_ge(mix_unit_used, 4 + n)
                        split(U_GU + 2 + n)
                if t >= 1:
                    evac_h2(t - 1)
                act_e.wait_ge(mix_done, t + 1)
                b = MIX_BANKS[t]
                sum_squares(SQ2, t, bank[:, b:b + 2, :].rearrange("p a n -> p (a n)"), mix_sq[:, :])
                act_e.wait_ge(x1_done, t + 1)
                sum_squares(SQ3, t, x_sb[:, t, :], mix_sq[:, :])
            evac_h2(TT - 1)

            def silu(f, par):
                act_e.wait_ge(gate_done, f + 1)
                if not isinstance(f, int) or f >= 2:
                    act_e.wait_ge(act_done, f - 1)
                nc.scalar.activation(silu_g[:, par, :], bank[:, GU_BANKS[par][0], :], ACT.Silu).then_inc(silu_done, 1)

            def split_gu(f, par):
                act_e.wait_ge(up_done, f + 1)
                for n in range(2):
                    u = U_GU + 4 + 2 * par + n
                    split(u, f * 8 + (16 * (u // RAW + 1) - 8 * par))

            def act_split(f, n):
                dst = act_hi[:, n, :] if n < 2 else lact_hi[:, n - 2, :]
                nc.scalar.copy(dst, act[:, f, :]).then_inc(act_hi_done, 1)

            for f in range(2):
                silu(f, f)
                split_gu(f, f)
            for f in range(2):
                act_e.wait_ge(act_done, f + 1)
                act_split(f, f)
            with act_e.Fori(1, FT // 2) as i:
                for par in range(2):
                    silu(i * 2 + par, par)
                    split_gu(i * 2 + par, par)

            act_e.wait_ge(act_done, FT)

            def down_turn(i, j):
                act_e.wait_ge(down_done, i * 4 + (j + 1))
                split(U_DOWN + 4 + j, i * 16 + 16 * ((U_DOWN + 4) // RAW + 1))
                if isinstance(i, int):
                    act_split(4 * i + j + 2, j % 2)
                else:
                    nc.scalar.copy(act_hi[:, j % 2, :], act[:, bass.ds(i * 4 + (j + 2), 1), :].rearrange(
                        "p o n -> p (o n)")).then_inc(act_hi_done, 1)

            with act_e.Fori(0, LOOP_DOWN // 4 - 1) as i:
                for j in range(4):
                    down_turn(i, j)
            for n in range(2):
                f = LOOP_DOWN - 4 + n
                act_e.wait_ge(down_done, f + 1)
                act_split(f + 2, n)
                split(U_DOWN + LOOP_DOWN + n)
            for n in range(LAST):
                act_split(LOOP_DOWN + n, 2 + n)
                if n + 2 < LAST:
                    split(U_DOWN + LOOP_DOWN + n + 2)

            for t in range(TT - 1):
                act_e.wait_ge(down_tile, t + 1)
                b = DOWN_BANKS[t]
                sum_squares(SQ4, t, bank[:, b:b + 2, :].rearrange("p a n -> p (a n)"), ff_sq[:, :])
            t, b = TT - 1, DOWN_BANKS[TT - 1]
            for h in range(2):
                act_e.wait_ge(down_tile, TT + h)
                nc.scalar.activation(ff_sq[:, 0:SEQ], bank[:, b + h, :], ACT.Square,
                                     accum_out=half_sum[:, h:h + 1]).then_inc(sq_done, 1)
                act_e.wait_ge(sq_done, norm_no(SQ4, t) + h)
                if h == 0:
                    nc.scalar.activation(half_eps[:, :], half_sum[:, 0:1], ACT.Identity, bias=eps[:, :],
                                         scale=1.0 / D).then_inc(half_eps_done, 1)
                    act_e.wait_ge(half_eps_done, 1)
            nc.scalar.activation(std[:, SQ4, t:t + 1], half_sum[:, 1:2], ACT.Sqrt, bias=half_eps[:, :],
                                 scale=1.0 / D).then_inc(std_done, 1)

        @block.vector
        def _(dve):
            def split(u, value=None):
                hi, lo = split_slot(u)
                dve.wait_ge(hi_done, u + 1 if value is None else value)
                nc.vector.tensor_tensor(lo[:, :, :], raw[u % RAW][:, :, :], hi[:, :, :],
                                        ALU.subtract).then_inc(lo_done, 1)

            def inverse_std(n, t):
                dve.wait_ge(std_done, norm_no(n, t))
                nc.vector.reciprocal(rstd[:, n, t:t + 1], std[:, n, t:t + 1]).then_inc(rstd_done, 1)
                dve.wait_ge(rstd_done, norm_no(n, t))

            nc.vector.memset(relb[BUCKETS:BUCKETS + 1, :], MASKED).then_inc(after_set, 1)
            for t in range(TT):
                inverse_std(SQ1, t)
                nc.vector.tensor_scalar(xn[:, t, :], x_sb[:, t, :], rstd[:, SQ1, t:t + 1], None,
                                        ALU.mult).then_inc(xn_done, 1)
            dve.wait_ge(small_in, 48)
            for k in range(KT):
                dve.wait_ge(hn_hi_done, k + 1)
                nc.vector.scalar_tensor_tensor(out=hn_lo[:, k, :], in0=bank[:, XT_BANKS[k], :],
                                               scalar=g_mix_c[:, k:k + 1], in1=hn_hi[:, k, :], op0=ALU.mult,
                                               op1=ALU.subtract).then_inc(hn_lo_done, 1)
                if k == KT // 2 - 1:
                    split(0)
            split(1)
            split(2)
            dve.wait_ge(wf_hi_done, 1)
            nc.vector.tensor_tensor(wf_hl[:, :, LO_COL:LO_COL + N_FOX], wf_raw[:, :, :], wf_hl[:, :, 0:N_FOX],
                                    ALU.subtract).then_inc(wf_lo_done, 1)
            split(3)

            def conv_tail(G):
                c, m = divmod(G - CONV_GROUP, 3)
                src = bank[:, PROJ[G % 2], :]
                dve.wait_ge(proj_done, G + 1)
                if m == 0:
                    dve.wait_ge(s_done, 8 * (PAIRS - 1))
                    nc.vector.memset(conv_u[:, 0:2], 0.0).then_inc(conv_step, 1)
                    nc.vector.tensor_copy(conv_c[:, :], src).then_inc(proj_read, 1)
                elif m == 1:
                    dve.wait_ge(proj_read, G)
                    dve.wait_ge(conv_step, 4 * c + 1)
                    nc.vector.tensor_tensor(conv_u[:, 2:2 + SEQ], src, conv_c[:, :], ALU.mult
                                            ).then_inc(proj_read, 1)
                    dve.wait_ge(proj_read, G + 1)
                    nc.vector.tensor_scalar(conv_y[:, :], conv_u[:, 2:2 + SEQ], conv_w_c[:, c, 2:3], None,
                                            ALU.mult).then_inc(conv_step, 1)
                    for n, tap in enumerate((1, 0)):
                        dve.wait_ge(conv_step, 4 * c + 2 + n)
                        nc.vector.scalar_tensor_tensor(out=conv_y[:, :], in0=conv_u[:, tap:tap + SEQ],
                                                       scalar=conv_w_c[:, c, tap:tap + 1], in1=conv_y[:, :],
                                                       op0=ALU.mult, op1=ALU.add).then_inc(conv_step, 1)
                else:
                    dve.wait_ge(conv_step, 4 * c + 4)
                    if c > 0:
                        dve.wait_ge(conv_lo, c)
                    nc.vector.tensor_tensor(conv_o[:, :], src, conv_y[:, :], ALU.mult).then_inc(proj_read, 1)

            def evac_lo(G):
                if G >= CONV_GROUP:
                    conv_tail(G)
                    return
                p, j = (0, G) if G < 3 else ((G - 4) // 3 + 1, (G - 4) % 3)
                src = bank[:, PROJ[G % 2], :]
                if j == 2:
                    dve.wait_ge(proj_done, G + 1)
                    if p >= 1:
                        dve.wait_ge(vT_done, p)
                    else:
                        dve.wait_ge(sq_done, TT)
                    nc.vector.tensor_copy(vT[:, :], src).then_inc(proj_read, 1)
                else:
                    dst = (q_hl, k_hl)[j][p % 2]
                    dve.wait_ge(proj_hi, 2 * p + j + 1)
                    for h in range(2):
                        last = nc.vector.scalar_tensor_tensor(
                            out=dst[DH:P, h, :], in0=src[DH * h:DH * (h + 1), :], scalar=SCALE if j == 0 else 1.0,
                            in1=dst[0:DH, h, :], op0=ALU.mult, op1=ALU.subtract)
                    last.then_inc(proj_read, 1)

            def forget_z():
                dve.wait_ge(proj_done, F_GROUP + 1)
                f_bank = PROJ[F_GROUP % 2]
                nc.vector.tensor_scalar(f_z[:, :], bank[0:N_FOX, f_bank, :], bf_c[:, :], None, ALU.add
                                        ).then_inc(f_z_part, 1)
                dve.wait_ge(f_z_part, 1)
                nc.vector.tensor_tensor(f_z[:, :], bank[LO_COL:LO_COL + N_FOX, f_bank, :], f_z[:, :], ALU.add
                                        ).then_inc(proj_read, 1)
                dve.wait_ge(proj_read, F_GROUP + 1)
                nc.vector.tensor_scalar(f_abs[:, :], f_z[:, :], -1.0, None, ALU.mult).then_inc(f_z_done, 1)
                dve.wait_ge(f_z_done, 1)
                nc.vector.tensor_tensor(f_abs[:, :], f_z[:, :], f_abs[:, :], ALU.max).then_inc(f_z_done, 1)

            def forget_cum():
                dve.wait_ge(f_log_done, 2)
                nc.vector.scalar_tensor_tensor(out=f_z[:, :], in0=f_z[:, :], scalar=0.0, in1=f_log[:, :],
                                               op0=ALU.min, op1=ALU.subtract).then_inc(f_z_done, 1)
                dve.wait_ge(f_z_done, 3)
                dve.wait_ge(consts_done, 9)
                nc.vector.tensor_tensor_scan(f_cum[:, :], f_one[:, :], f_z[:, :], 0.0, ALU.mult,
                                             ALU.subtract).then_inc(f_cum_done, 1)

            def evac_v(p):
                dve.wait_ge(v_hi_done, p + 1)
                nc.vector.tensor_tensor(v_hl[p % 2][:, :, :, DH:P],
                                        bank[:, VTBANK, :].rearrange("p (j h d) -> p j h d", j=TT, h=2),
                                        v_hl[p % 2][:, :, :, 0:DH], ALU.subtract).then_inc(v_lo_done, 1)

            def evac_pT(g):
                i = g % 4
                dve.wait_ge(pT_hi_done, g + 1)
                nc.vector.tensor_tensor(pT_lo[:, 0:i + 1, P * i:P * (i + 1)],
                                        bank[:, TBANK[g % 2], 0:P * (i + 1)].rearrange("p (j q) -> p j q", q=P),
                                        pT_hi[:, 0:i + 1, P * i:P * (i + 1)], ALU.subtract).then_inc(pT_lo_done, 1)

            def sum_o(head):
                p, h = divmod(head, 2)
                dve.wait_ge(o_top_done, head + 1)
                if h == 0 and p >= 1:
                    dve.wait_ge(o_lo, p)
                nc.vector.tensor_tensor(o_sum[DH * h:DH * (h + 1), :], bank[0:DH, OBANK, :], o_top[:, :],
                                        ALU.add).then_inc(o_summed, 1)

            def evac_o(p):
                dve.wait_ge(o_hi, p + 1)
                nc.vector.tensor_tensor(cat_lo[:, p, :], o_sum[:, :], cat_hi[:, p, :], ALU.subtract
                                        ).then_inc(o_lo, 1)

            evac_lo(group(0, 0))
            evac_lo(group(0, 1))
            dve.wait_ge(rel_done, 1)
            nc.vector.tensor_copy(rel_row[:, 0:SEQ], bank[0:N_MOBA, OBANK, :]).then_inc(rel_copied, 1)
            nc.vector.tensor_copy(rel_row[:, SEQ:REL], bank[0:N_MOBA, VTBANK, 0:REL - SEQ]).then_inc(rel_copied, 1)
            evac_lo(group(0, 2))
            split(4)
            forget_z()

            conv_lo_at = {6: 0, 9: 1}
            for g in range(STEPS + 3):
                p, s = divmod(g, 8)
                hi_kinds = [G for G in finished(g - 2) if has_hi(G)]
                if s == 7:
                    for G in hi_kinds:
                        evac_lo(G)
                if g < STEPS:
                    i, h = g % 4, (g // 4) % 2
                    n = P * (i + 1)
                    dve.wait_ge(s_done, g + 1)
                    if s == 0:
                        dve.wait_ge(bias_in[p % 2], 32 * (p // 2 + 1))
                    if g >= 2:
                        dve.wait_ge(exp_done, g - 1)
                    bias_ap = bias[:, p % 2, h, 0:n]
                    if p < MOBA_PAIRS:
                        bias_ap = bias_ap[:, ::-1]
                    nc.vector.tensor_tensor_reduce(
                        out=logits[:, g % 2, 0:n], in0=bank[:, SBANK[g % 2], 0:n], in1=bias_ap,
                        scale=-1.0, scalar=3.0e38, op0=ALU.add, op1=ALU.min,
                        accum_out=neg_max[:, g:g + 1]).then_inc(biased, 1)
                if g >= 3:
                    evac_pT(g - 3)
                for G in finished(g - 1):
                    if not has_hi(G):
                        evac_lo(G)
                if s != 7:
                    for G in hi_kinds:
                        evac_lo(G)
                for u in splits_at(g - 1):
                    split(u)
                if p < PAIRS and s == 3:
                    evac_v(p)
                if g == 5:
                    forget_cum()
                if g < STEPS:
                    dve.wait_ge(exp_done, g + 1)
                    nc.vector.reciprocal(row_inv[:, g:g + 1], row_sum[:, g:g + 1]).then_inc(inv_done, 1)
                    dve.wait_ge(inv_done, g + 1)
                    nc.vector.tensor_scalar(probs[g % 3][:, 0:n], probs[g % 3][:, 0:n], row_inv[:, g:g + 1], None,
                                            ALU.mult).then_inc(normed, 1)
                if g >= 8 and s in (0, 3):
                    sum_o((g - 7) // 4)
                if g >= 13 and g % 8 == 5:
                    evac_o((g - 13) // 8)
                if g - 8 * (PAIRS - 1) in conv_lo_at:
                    c = conv_lo_at[g - 8 * (PAIRS - 1)]
                    dve.wait_ge(conv_hi, c + 1)
                    nc.vector.tensor_tensor(cat_lo[:, 6 + c, :], conv_o[:, :], cat_hi[:, 6 + c, :], ALU.subtract
                                            ).then_inc(conv_lo, 1)
            split(U_WOUT + 6)
            sum_o(2 * PAIRS - 1)
            split(U_WOUT + 7)
            evac_o(PAIRS - 1)
            dve.wait_ge(conv_lo, 2)
            split(U_GU)
            split(U_GU + 1)

            def evac_h2(t):
                for b in range(2):
                    dve.wait_ge(h2_hi, 2 * t + b + 1)
                    nc.vector.tensor_tensor(hn_lo[:, 4 * b:4 * b + 4, P * t:P * (t + 1)],
                                            bank[:, TBANK[b], :].rearrange("p (k q) -> p k q", q=P),
                                            hn_hi[:, 4 * b:4 * b + 4, P * t:P * (t + 1)], ALU.subtract
                                            ).then_inc(h2_lo, 1)

            for t in range(TT):
                if t == TT - 1:
                    split(U_GU + 2)
                    split(U_GU + 3)
                if t >= 1:
                    evac_h2(t - 1)
                if t == 0:
                    dve.wait_ge(g_post_mix_in, 16)
                inverse_std(SQ2, t)
                b = MIX_BANKS[t]
                y = mix_y[:, t % 2, :]
                if t >= 2:
                    dve.wait_ge(h2T_done, 2 * (t - 1))
                nc.vector.scalar_tensor_tensor(out=y, in0=bank[:, b:b + 2, :].rearrange("p a n -> p (a n)"),
                                               scalar=rstd[:, SQ2, t:t + 1], in1=g_post_mix_b[:, :], op0=ALU.mult,
                                               op1=ALU.mult).then_inc(mix_normed, 1)
                dve.wait_ge(mix_normed, t + 1)
                nc.vector.tensor_tensor(x_sb[:, t, :], x_sb[:, t, :], y, ALU.add).then_inc(x1_done, 1)
                inverse_std(SQ3, t)
                if t == 0:
                    dve.wait_ge(g_pre_ffn_in, 16)
                nc.vector.scalar_tensor_tensor(out=y, in0=x_sb[:, t, :], scalar=rstd[:, SQ3, t:t + 1],
                                               in1=g_pre_ffn_b[:, :], op0=ALU.mult, op1=ALU.mult
                                               ).then_inc(h2_done, 1)
            evac_h2(TT - 1)

            def gated(f, par):
                dve.wait_ge(silu_done, f + 1)
                dve.wait_ge(up_done, f + 1)
                dst = act[:, f, :] if isinstance(f, int) else \
                    act[:, bass.ds(f, 1), :].rearrange("p o n -> p (o n)")
                nc.vector.tensor_tensor(dst, bank[:, GU_BANKS[par][1], :], silu_g[:, par, :], ALU.mult
                                        ).then_inc(act_done, 1)
                for n in range(2):
                    split(U_GU + 4 + 2 * par + n, f * 2 + (U_GU + 4 + n + 1))

            def act_split(f, n, count):
                hi = act_hi[:, n, :] if n < 2 else lact_hi[:, n - 2, :]
                lo = act_lo[:, n, :] if n < 2 else lact_lo[:, n - 2, :]
                src = act[:, f, :] if isinstance(f, int) else act[:, bass.ds(f, 1), :].rearrange("p o n -> p (o n)")
                dve.wait_ge(act_hi_done, count)
                nc.vector.tensor_tensor(lo, src, hi, ALU.subtract).then_inc(act_lo_done, 1)

            for f in range(2):
                gated(f, f)
            for f in range(2):
                act_split(f, f, f + 1)
            with dve.Fori(1, FT // 2) as i:
                for par in range(2):
                    gated(i * 2 + par, par)
            dve.wait_ge(act_done, FT)
            with dve.Fori(0, LOOP_DOWN // 4 - 1) as i:
                for j in range(4):
                    split(U_DOWN + 4 + j, i * 4 + (U_DOWN + 4 + j + 1))
                    act_split(i * 4 + (j + 2), j % 2, i * 4 + (j + 3))
            for n in range(2):
                f = LOOP_DOWN - 2 + n
                act_split(f, n, f + 1)
                split(U_DOWN + LOOP_DOWN + n)
            for n in range(LAST):
                act_split(LOOP_DOWN + n, 2 + n, LOOP_DOWN + n + 1)
                if n + 2 < LAST:
                    split(U_DOWN + LOOP_DOWN + n + 2)

            dve.wait_ge(g_ffn_in, 16)
            dve.wait_ge(act_lo_done, FT)
            for t in range(TT - 1):
                inverse_std(SQ4, t)
                b = DOWN_BANKS[t]
                nc.vector.scalar_tensor_tensor(out=ff_y[:, t, :], in0=bank[:, b:b + 2, :].rearrange("p a n -> p (a n)"),
                                               scalar=rstd[:, SQ4, t:t + 1], in1=g_post_ffn_b[:, :], op0=ALU.mult,
                                               op1=ALU.mult).then_inc(ff_normed, 1)
                dve.wait_ge(ff_normed, t + 1)
                nc.vector.tensor_tensor(ff_y[:, t, :], ff_y[:, t, :], x_sb[:, t, :], ALU.add).then_inc(y_done, 1)
            t, b = TT - 1, DOWN_BANKS[TT - 1]
            halves = (slice(0, SEQ), slice(SEQ, D))
            for h, c in enumerate(halves):
                dve.wait_ge(sq_done, norm_no(SQ4, t) + h)
                nc.vector.tensor_tensor(ff_y[:, t, c], bank[:, b + h, :], g_post_ffn_b[:, c], ALU.mult
                                        ).then_inc(half_scaled, 1)
            inverse_std(SQ4, t)
            dve.wait_ge(half_scaled, 2)
            for c in halves:
                nc.vector.scalar_tensor_tensor(out=ff_y[:, t, c], in0=ff_y[:, t, c], scalar=rstd[:, SQ4, t:t + 1],
                                               in1=x_sb[:, t, c], op0=ALU.mult, op1=ALU.add).then_inc(y_done, 1)

        @block.tensor
        def _(pe):
            def product(out_ap, st, mv, first, last):
                (sh, sl), (mh, ml) = st, mv
                nc.tensor.matmul(out_ap, sh, mh, start=first, stop=False)
                nc.tensor.matmul(out_ap, sh, ml, start=False, stop=False)
                return nc.tensor.matmul(out_ap, sl, mh, start=False, stop=last)

            pe.wait_ge(consts_done, 5)
            for t in range(TT):
                pe.wait_ge(xn_done, t + 1)
                for k in range(6):
                    mm = nc.tensor.transpose(bank[:, XT_BANKS[k], P * t:P * (t + 1)],
                                             xn[:, t, P * k:P * (k + 1)], ident[:, :])
                    if t == TT - 1:
                        mm.then_inc(xT_done, 1)

            def proj_step(G, u, k):
                if k == 0:
                    pe.wait_ge(lo_done, u + 1)
                    if G >= 2:
                        pe.wait_ge(proj_read, G - 1)
                hi, lo = w_hi[u % 4], w_lo[u % 4]
                mm = product(bank[:, PROJ[G % 2], :], (hi[:, k, :], lo[:, k, :]), (hn_hi[:, k, :], hn_lo[:, k, :]),
                             k == 0, k == KT - 1)
                if k == KT - 1:
                    mm.then_inc(proj_done, 1)

            def relative_rows():
                pe.wait_ge(tables_in, 32)
                pe.wait_ge(after_set, 1)
                nc.tensor.matmul(bank[0:N_MOBA, OBANK, :], relb[:, :], onehot[:, 0:SEQ], start=True, stop=True)
                nc.tensor.matmul(bank[0:N_MOBA, VTBANK, 0:REL - SEQ], relb[:, :], onehot[:, SEQ:REL], start=True,
                                 stop=True).then_inc(rel_done, 1)

            def pass_of(j, ks, weight, part, first=False, last=False):
                for k in ks:
                    mm = nc.tensor.matmul(bank[:, PROJ[j], :], weight[j][:, k, :], part[:, k, :],
                                          start=first and k == ks[0], stop=last and k == ks[-1])
                return mm

            early, late = range(KT // 2), range(KT // 2, KT)
            pe.wait_ge(hi_done, 1)
            for k in early:
                pe.wait_ge(hn_hi_done, k + 1)
                pass_of(0, [k], w_hi, hn_hi, first=k == 0)
                if k >= 1:
                    pe.wait_ge(hn_lo_done, k)
                    pass_of(0, [k - 1], w_hi, hn_lo)
                if 1 <= k <= 2:
                    for t in range(TT):
                        mm = nc.tensor.transpose(bank[:, XT_BANKS[5 + k], P * t:P * (t + 1)],
                                                 xn[:, t, P * (5 + k):P * (6 + k)], ident[:, :])
                    mm.then_inc(xT_done, 1)
            pe.wait_ge(hn_lo_done, KT // 2)
            pass_of(0, [early[-1]], w_hi, hn_lo)
            pe.wait_ge(hi_done, 2)
            pass_of(1, early, w_hi, hn_hi, first=True)
            pass_of(1, early, w_hi, hn_lo)
            pe.wait_ge(lo_done, 1)
            pass_of(0, early, w_lo, hn_hi)
            for k in late:
                pe.wait_ge(hn_hi_done, k + 1)
                pass_of(0, [k], w_hi, hn_hi)
                pass_of(0, [k], w_lo, hn_hi)
                pass_of(1, [k], w_hi, hn_hi)
            for k in late:
                pe.wait_ge(hn_lo_done, k + 1)
                mm = pass_of(0, [k], w_hi, hn_lo, last=k == KT - 1)
            mm.then_inc(proj_done, 1)
            pass_of(1, late, w_hi, hn_lo)
            pe.wait_ge(lo_done, 2)
            pass_of(1, range(KT), w_lo, hn_hi, last=True).then_inc(proj_done, 1)
            relative_rows()
            for k in range(KT):
                proj_step(group(0, 2), 2, k)
            pe.wait_ge(wf_lo_done, 1)
            pe.wait_ge(proj_read, F_GROUP - 1)
            for k in range(KT):
                for part in (hn_hi, hn_lo):
                    mm = nc.tensor.matmul(bank[0:LO_COL + N_FOX, PROJ[F_GROUP % 2], :], wf_hl[:, k, :], part[:, k, :],
                                          start=k == 0 and part is hn_hi, stop=k == KT - 1 and part is hn_lo)
            mm.then_inc(proj_done, 1)

            def logits_step(g):
                p, s = divmod(g, 8)
                h, i = divmod(s, 4)
                n = P * (i + 1)
                if s == 0:
                    pe.wait_ge(proj_read, group(p, 1) + 1)
                    pe.wait_ge(swapped[p % 2], 32 * (p // 2 + 1))
                if g >= 2:
                    pe.wait_ge(biased, g - 1)
                b = SBANK[g % 2]
                q = slice(P * i, P * (i + 1))
                k_ap = k_hl[p % 2][:, h, 0:n]
                nc.tensor.matmul(bank[:, b, 0:n], q_hl[p % 2][:, h, q], k_ap, start=True, stop=False,
                                 skip_group_check=True)
                mm = nc.tensor.matmul(bank[:, b, 0:n], q_lh[p % 2][:, h, q], k_ap, start=False,
                                      stop=p < MOBA_PAIRS, skip_group_check=True)
                if p < MOBA_PAIRS:
                    mm.then_inc(s_done, 1)
                    return
                nc.tensor.matmul(bank[:, b, P * i:n], ident_b[:, :], mask_b[:, :], start=False, stop=True,
                                 skip_group_check=True).then_inc(s_done, 1)

            def transpose_step(g):
                i = g % 4
                pe.wait_ge(normed, g + 1)
                if g >= 2:
                    pe.wait_ge(pT_lo_done, g - 1)
                for j in range(i + 1):
                    mm = nc.tensor.transpose(bank[:, TBANK[g % 2], P * j:P * (j + 1)],
                                             probs[g % 3][:, P * j:P * (j + 1)], ident[:, :])
                mm.then_inc(t_done, 1)

            def pv(head):
                p, h = divmod(head, 2)
                pe.wait_ge(pT_lo_done, 4 * head + 4)
                pe.wait_ge(v_lo_done, p + 1)
                if head >= 1:
                    pe.wait_ge(o_summed, head)
                for j in range(TT):
                    for part in (pT_hi, pT_lo):
                        mm = nc.tensor.matmul(bank[:, OBANK, P * j:SEQ], v_hl[p % 2][:, j, h, :],
                                              part[:, j, P * j:SEQ], start=j == 0 and part is pT_hi,
                                              stop=j == TT - 1 and part is pT_lo, skip_group_check=True)
                mm.then_inc(pv_done, 1)

            def v_tokens(p):
                pe.wait_ge(proj_read, group(p, 2) + 1)
                if p >= 1:
                    pe.wait_ge(v_lo_done, p)
                for j in range(TT):
                    mm = nc.tensor.transpose(bank[:, VTBANK, P * j:P * (j + 1)], vT[:, P * j:P * (j + 1)],
                                             ident[:, :])
                mm.then_inc(vT_done, 1)

            def mix_part(t, n):
                k = WOUT_ORDER[n]
                if t == 0:
                    pe.wait_ge(lo_done, U_WOUT + n + 1)
                    if k < PAIRS:
                        pe.wait_ge(o_lo, k + 1)
                    else:
                        pe.wait_ge(conv_lo, k - PAIRS + 1)
                hi, lo = split_slot(U_WOUT + n)
                for h in range(2):
                    c = slice(4 * h, 4 * h + 4)
                    mm = product(bank[:, MIX_BANKS[t] + h, :],
                                 (cat_hi[:, k, P * t:P * (t + 1)], cat_lo[:, k, P * t:P * (t + 1)]),
                                 (hi[:, c, :].rearrange("p k n -> p (k n)"), lo[:, c, :].rearrange("p k n -> p (k n)")),
                                 n == 0, n == KT - 1)
                if t == TT - 1 and n < 7:
                    mm.then_inc(mix_unit_used, 1)
                if n == KT - 1:
                    mm.then_inc(mix_done, 1)

            for g in range(STEPS):
                p, s = divmod(g, 8)
                logits_step(g)
                parts = 3 if p < PAIRS - 1 else 6
                for m in range(parts):
                    n = parts * s + m
                    proj_step(group(p + 1, 0) + n // 8, 3 * (p + 1) + n // 8, n % 8)
                    if m == parts * 2 // 3:
                        if g >= 6 and (g - 6) % 4 == 0:
                            pv((g - 6) // 4)
                        if g >= 2:
                            transpose_step(g - 2)
                if s == 1:
                    v_tokens(p)

            pe.wait_ge(biased, STEPS)
            for n in range(KT):
                mix_part(0, n)
                if n < 2:
                    transpose_step(STEPS - 2 + n)
                if n == 4:
                    pv(2 * PAIRS - 1)

            def h2_tokens(t):
                pe.wait_ge(h2_done, t + 1)
                for b in range(2):
                    if t >= 1:
                        pe.wait_ge(h2_lo, 2 * t - 1 + b)
                    else:
                        pe.wait_ge(pT_lo_done, STEPS)
                    for k in range(4 * b, 4 * b + 4):
                        mm = nc.tensor.transpose(bank[:, TBANK[b], P * (k % 4):P * (k % 4 + 1)],
                                                 mix_y[:, t % 2, P * k:P * (k + 1)], ident[:, :])
                    mm.then_inc(h2T_done, 1)

            for t in range(1, TT):
                if t == 1:
                    pe.wait_ge(proj_read, GROUPS)
                else:
                    pe.wait_ge(mix_normed, t - 1)
                for n in range(KT):
                    mix_part(t, n)
                    if n == (5 if t == TT - 1 else 6):
                        h2_tokens(t - 1)

            def ff_half(slot, b, tokens):
                for k in range(KT):
                    mm = product(bank[:, b, tokens], (slot[0][:, k, :], slot[1][:, k, :]),
                                 (hn_hi[:, k, tokens], hn_lo[:, k, tokens]), k == 0, k == KT - 1)
                return mm

            pe.wait_ge(lo_done, U_GU + 2)
            pe.wait_ge(h2_lo, 2 * (TT - 1))
            pe.wait_ge(o_lo, PAIRS)
            pe.wait_ge(v_lo_done, PAIRS)
            early, late, every = slice(0, SEQ - P), slice(SEQ - P, SEQ), slice(0, SEQ)
            g0, u0 = split_slot(U_GU), split_slot(U_GU + 1)
            g1, u1 = split_slot(U_GU + 2), split_slot(U_GU + 3)
            ff_half(g0, GU_BANKS[0][0], early)
            ff_half(u0, GU_BANKS[0][1], early)
            h2_tokens(TT - 1)
            pe.wait_ge(mix_normed, 3)
            pe.wait_ge(lo_done, U_GU + 3)
            ff_half(g1, GU_BANKS[1][0], early)
            pe.wait_ge(h2_lo, 2 * TT)
            ff_half(g0, GU_BANKS[0][0], late).then_inc(gate_done, 1)
            ff_half(u0, GU_BANKS[0][1], late).then_inc(up_done, 1)
            ff_half(g1, GU_BANKS[1][0], late).then_inc(gate_done, 1)
            pe.wait_ge(lo_done, U_GU + 4)
            ff_half(u1, GU_BANKS[1][1], every).then_inc(up_done, 1)
            with pe.Fori(1, FT // 2) as i:
                for par in range(2):
                    pe.wait_ge(lo_done, i * 4 + (U_GU + 2 * par + 2))
                    pe.wait_ge(act_done, i * 2 + (par - 1))
                    for n, done in enumerate((gate_done, up_done)):
                        s = 2 * par + n
                        ff_half((w_hi[s], w_lo[s]), GU_BANKS[par][n], every).then_inc(done, 1)

            def down(units, acts, t, first, last, halves=range(2)):
                for h in halves:
                    c = slice(4 * h, 4 * h + 4)
                    mm = product(bank[:, DOWN_BANKS[t] + h, :],
                                 (acts[0][:, P * t:P * (t + 1)], acts[1][:, P * t:P * (t + 1)]),
                                 (units[0][:, c, :].rearrange("p k n -> p (k n)"),
                                  units[1][:, c, :].rearrange("p k n -> p (k n)")), first, last)
                return mm

            pe.wait_ge(mix_normed, TT)

            def down_turn(j, count, first):
                pe.wait_ge(act_lo_done, count)
                for t in range(TT):
                    if first and t >= 2:
                        pe.wait_ge(act_done, FT - TT + 1 + t)
                    mm = down((w_hi[j], w_lo[j]), (act_hi[:, j % 2, :], act_lo[:, j % 2, :]), t, first, False)
                mm.then_inc(down_done, 1)

            for j in range(4):
                pe.wait_ge(lo_done, U_DOWN + j + 1)
                down_turn(j, j + 1, j == 0)
            with pe.Fori(1, LOOP_DOWN // 4) as i:
                for j in range(4):
                    pe.wait_ge(lo_done, i * 4 + (U_DOWN + j + 1))
                    down_turn(j, i * 4 + (j + 1), False)
            for t in range(TT):
                for halves in ((range(2),) if t < TT - 1 else ((0,), (1,))):
                    for n in range(LAST):
                        if t == 0:
                            pe.wait_ge(lo_done, U_DOWN + LOOP_DOWN + n + 1)
                            pe.wait_ge(act_lo_done, LOOP_DOWN + n + 1)
                        mm = down((last_hi[n], last_lo[n]), (lact_hi[:, n, :], lact_lo[:, n, :]), t, False,
                                  n == LAST - 1, halves)
                    mm.then_inc(down_tile, 1)


def bucket_table():
    import math
    import numpy as np
    dist = np.maximum(np.arange(REL) - (P - 1), 0)
    exact = BUCKETS // 2
    far = np.log(np.maximum(dist, 1).astype(np.float32) / np.float32(exact)) / np.float32(math.log(128 / exact))
    large = np.minimum(exact + (far * np.float32(BUCKETS - exact)).astype(np.int32), BUCKETS - 1)
    bucket = np.where(dist < exact, dist, large)
    bucket = np.where(np.arange(REL) < P - 1, BUCKETS, bucket)
    return (np.arange(BUCKETS + 1)[:, None] == bucket[None, :]).astype(np.float32)


def kernel(x, w_in, b_f, conv_w, w_out, rel_bias, g_pre_mix, g_post_mix, g_pre_ffn, g_post_ffn, w_gate, w_up,
           w_down):
    import numpy as np
    import concourse.bacc as bacc
    from concourse.bass_utils import run_bass_kernel_spmd

    def units(w):
        w = np.asarray(w)
        n = w.shape[1] // P
        return np.ascontiguousarray(w.reshape(KT, P, n, P).transpose(2, 1, 0, 3).reshape(n, P, KT * P))

    w = np.asarray(w_in)[0]
    fox0 = 3 * MOBA_W
    conv0 = fox0 + 3 * FOX_W + N_FOX
    starts = [base + P * p + j * MOBA_W for base in (0, fox0) for p in range(MOBA_PAIRS) for j in range(3)]
    starts += [conv0 + P * c + CONV_CH * m for c in range(2) for m in (1, 2, 0)]
    tiles = np.concatenate([w[:, s:s + P] for s in starts], axis=1)
    w_f = w[:, fox0 + 3 * FOX_W:conv0].reshape(KT, P, N_FOX).transpose(1, 0, 2)
    arrays = {
        "x": np.asarray(x)[0],
        "w_in_units": units(tiles),
        "w_f": w_f,
        "b_f": np.asarray(b_f).reshape(N_FOX, 1),
        "conv_w": np.asarray(conv_w)[0].reshape(3, 2, P).transpose(2, 1, 0),
        "w_out": np.asarray(w_out)[0],
        "rel_bias": np.asarray(rel_bias),
        "bucket_onehot": bucket_table(),
        "g_pre_mix": np.asarray(g_pre_mix).reshape(KT, P).T,
        "g_post_mix": np.asarray(g_post_mix).reshape(D),
        "g_pre_ffn": np.asarray(g_pre_ffn).reshape(D),
        "g_post_ffn": np.asarray(g_post_ffn).reshape(D),
        "w_gate_units": units(np.asarray(w_gate)[0]),
        "w_up_units": units(np.asarray(w_up)[0]),
        "w_down": np.asarray(w_down)[0],
    }
    nc = bacc.Bacc("TRN2", target_bir_lowering=False, num_devices=1)
    ins, args = {}, []
    for name, a in arrays.items():
        a = np.ascontiguousarray(a)
        ins[f"in_{name}"] = a
        args.append(nc.dram_tensor(f"in_{name}", a.shape, mybir.dt.from_np(a.dtype), kind="ExternalInput").ap())
    out = nc.dram_tensor("out", (SEQ, D), F32, kind="ExternalOutput").ap()
    hybrid_block(nc, *args, out)
    r = run_bass_kernel_spmd(nc, [ins], core_ids=[0])
    return r.results[0]["out"].reshape(1, SEQ, D)
```
